# Optimizing a Trainium2 kernel written in Bass

```python
import math
import jax
import jax.numpy as jnp
from jax import lax
import numpy as np
import jax, jax.numpy as jnp

D_MODEL = 1024
BATCH = 1
SEQ = 512
DEPTH = 1

MIX_WIDTH = D_MODEL
MLSTM_WIDTH = MIX_WIDTH // 2
ATTN_WIDTH = MIX_WIDTH - MLSTM_WIDTH
MLSTM_HEADS = 4
MLSTM_HEAD_DIM = MLSTM_WIDTH // MLSTM_HEADS
MLSTM_QKV_BLOCK = 4
MLSTM_CONV = 5
MLSTM_CHUNK = 64
ATTN_HEAD_DIM = 64
ATTN_HEADS = ATTN_WIDTH // ATTN_HEAD_DIM
DILATED_PATTERNS = ((128, 1), (512, 4), (2048, 16))
ATTN_BLOCK = 64
REL_BUCKETS = 32
REL_MAX_DIST = 1024
N_EXPERTS = 16
EC_CAPACITY_FACTOR = 2
D_FF_EXPERT = 2 * D_MODEL
NORM_EPS = 1e-6
N_MOD = 6
PROJ_WIDTHS = (MLSTM_WIDTH, MLSTM_WIDTH, MLSTM_HEADS, MLSTM_HEADS, MLSTM_HEADS, MLSTM_HEADS,
               ATTN_WIDTH, ATTN_WIDTH, ATTN_WIDTH)
PROJ_TOTAL = sum(PROJ_WIDTHS)


def rms_norm(x, g):
    xf = x.astype(jnp.float32)
    y = xf * lax.rsqrt(jnp.mean(xf * xf, axis=-1, keepdims=True) + NORM_EPS)
    return (y * g.astype(jnp.float32)).astype(x.dtype)

def t5_bucket(rel):
    half = REL_BUCKETS // 2
    exact = half // 2
    n = jnp.abs(rel)
    log_ratio = jnp.log(jnp.maximum(n, 1).astype(jnp.float32) / exact) / math.log(REL_MAX_DIST / exact)
    large = jnp.minimum(exact + (log_ratio * (half - exact)).astype(jnp.int32), half - 1)
    return jnp.where(rel > 0, half, 0) + jnp.where(n < exact, n, large)

def dilated_window_attention(q, k, v, rel_bias, window, dilation):
    B, S, H, E = q.shape
    half = window // (2 * dilation)
    L = S // dilation
    nb = -(-L // ATTN_BLOCK)
    pad = nb * ATTN_BLOCK - L

    def phases(t):
        return t.reshape(B, L, dilation, H, E).transpose(0, 2, 3, 1, 4).reshape(B * dilation, H, L, E)

    qb = jnp.pad(phases(q), ((0, 0), (0, 0), (0, pad), (0, 0))).reshape(B * dilation, H, nb, ATTN_BLOCK, E)

    def key_blocks(t):
        tp = jnp.pad(phases(t), ((0, 0), (0, 0), (ATTN_BLOCK, pad + ATTN_BLOCK), (0, 0)))
        tp = tp.reshape(B * dilation, H, nb + 2, ATTN_BLOCK, E)
        return jnp.concatenate([tp[:, :, 0:nb], tp[:, :, 1:nb + 1], tp[:, :, 2:nb + 2]], axis=3)

    kb, vb = key_blocks(k), key_blocks(v)
    qi = jnp.arange(ATTN_BLOCK)[:, None]
    kj = jnp.arange(3 * ATTN_BLOCK)[None, :] - ATTN_BLOCK
    rel = kj - qi
    key_pos = jnp.arange(nb)[:, None] * ATTN_BLOCK + kj
    valid = (jnp.abs(rel) <= half)[None] & ((key_pos >= 0) & (key_pos < L))[:, None, :]
    bias = rel_bias[t5_bucket(rel * dilation)].transpose(2, 0, 1).astype(jnp.float32)
    logits = jnp.einsum('nhcqe,nhcke->nhcqk', qb, kb).astype(jnp.float32) / math.sqrt(E) + bias[:, None]
    logits = jnp.where(valid, logits, -jnp.inf)
    lse = jax.nn.logsumexp(logits, axis=-1)
    p = jnp.exp(logits - lse[..., None]).astype(v.dtype)
    o = jnp.einsum('nhcqk,nhcke->nhcqe', p, vb)
    o = o.reshape(B * dilation, H, nb * ATTN_BLOCK, E)[:, :, :L]
    o = o.reshape(B, dilation, H, L, E).transpose(0, 3, 1, 2, 4).reshape(B, S, H, E)
    lse = lse.reshape(B * dilation, H, nb * ATTN_BLOCK)[:, :, :L]
    lse = lse.reshape(B, dilation, H, L).transpose(0, 3, 1, 2).reshape(B, S, H)
    return o, lse

def dilated_attention_mixer(a_q, a_k, a_v, q_norm_g, k_norm_g, rel_bias):
    B, S, _ = a_q.shape
    heads = lambda t: t.reshape(B, S, ATTN_HEADS, ATTN_HEAD_DIM)
    q = rms_norm(heads(a_q), q_norm_g)
    k = rms_norm(heads(a_k), k_norm_g)
    v = heads(a_v)
    outs, lses = zip(*[dilated_window_attention(q, k, v, rel_bias, w, d) for w, d in DILATED_PATTERNS])
    weights = jax.nn.softmax(jnp.stack(lses), axis=0)
    o = jnp.sum(weights[..., None] * jnp.stack(outs).astype(jnp.float32), axis=0)
    return o.reshape(B, S, ATTN_WIDTH).astype(a_q.dtype)

def mlstm_chunkwise(q, k, v, i_pre, log_f):
    B, H, S, E = q.shape
    NC = S // MLSTM_CHUNK
    ch = lambda t: t.reshape((B, H, NC, MLSTM_CHUNK) + t.shape[3:])
    q, k, v, i_pre, log_f = ch(q), ch(k), ch(v), ch(i_pre), ch(log_f)
    b = jnp.cumsum(log_f, axis=-1)
    g = b[..., -1]
    a = g[..., None] - b + i_pre

    def step(carry, xs):
        C, n, m = carry
        kc, vc, ac, gc = xs
        m_new = jnp.maximum(gc + m, jnp.max(ac, axis=-1))
        w = jnp.exp(ac - m_new[..., None])
        decay = jnp.exp(gc + m - m_new)
        C_new = decay[..., None, None] * C + jnp.einsum('bhl,bhld,bhle->bhde', w, kc, vc)
        n_new = decay[..., None] * n + jnp.einsum('bhl,bhld->bhd', w, kc)
        return (C_new, n_new, m_new), (C, n, m)

    init = (jnp.zeros((B, H, E, E), jnp.float32), jnp.zeros((B, H, E), jnp.float32), jnp.zeros((B, H), jnp.float32))
    xs = tuple(jnp.moveaxis(t, 2, 0) for t in (k, v, a, g))
    _, (C_prev, n_prev, m_prev) = lax.scan(step, init, xs)
    C_prev = jnp.moveaxis(C_prev, 0, 2)
    n_prev = jnp.moveaxis(n_prev, 0, 2)
    m_prev = jnp.moveaxis(m_prev, 0, 2)

    lower = jnp.tril(jnp.ones((MLSTM_CHUNK, MLSTM_CHUNK), dtype=bool))
    D = jnp.where(lower, b[..., :, None] - b[..., None, :] + i_pre[..., None, :], -jnp.inf)
    inter = b + m_prev[..., None]
    m_t = jnp.maximum(inter, jnp.max(D, axis=-1))
    w_intra = jnp.exp(D - m_t[..., None]) * jnp.einsum('bhcte,bhcje->bhctj', q, k)
    w_inter = jnp.exp(inter - m_t)
    num = w_inter[..., None] * jnp.einsum('bhcte,bhced->bhctd', q, C_prev) + jnp.einsum('bhctj,bhcjd->bhctd', w_intra, v)
    den = w_inter * jnp.einsum('bhcte,bhce->bhct', q, n_prev) + jnp.sum(w_intra, axis=-1)
    h = num / jnp.maximum(jnp.abs(den), jnp.exp(-m_t))[..., None]
    return h.reshape(B, H, S, E)

def mlstm_mixer(x_m, o_pre, i_fw, f_fw, i_bw, f_bw, conv_w, conv_b, w_q_blk, w_k_blk, w_v_blk,
                b_igate, b_fgate, out_norm_g, skip):
    B, S, _ = x_m.shape
    xc = lax.conv_general_dilated(x_m, conv_w[:, None, :], window_strides=(1,),
                                  padding=((MLSTM_CONV // 2, MLSTM_CONV // 2),),
                                  dimension_numbers=('NWC', 'WIO', 'NWC'),
                                  feature_group_count=MLSTM_WIDTH) + conv_b
    xc = jax.nn.silu(xc)

    def blockdiag(t, w):
        y = jnp.einsum('bsgi,gij->bsgj', t.reshape(B, S, -1, MLSTM_QKV_BLOCK), w)
        return y.reshape(B, S, MLSTM_HEADS, MLSTM_HEAD_DIM).transpose(0, 2, 1, 3).astype(jnp.float32)

    q = blockdiag(xc, w_q_blk)
    k = blockdiag(xc, w_k_blk) / math.sqrt(MLSTM_HEAD_DIM)
    v = blockdiag(x_m, w_v_blk)
    gate = lambda t, bias: (t.astype(jnp.float32) + bias.astype(jnp.float32)).transpose(0, 2, 1)
    i_f, logf_f = gate(i_fw, b_igate[0]), jax.nn.log_sigmoid(gate(f_fw, b_fgate[0]))
    i_b, logf_b = gate(i_bw, b_igate[1]), jax.nn.log_sigmoid(gate(f_bw, b_fgate[1]))
    flip = lambda t: jnp.flip(t, axis=2)
    h_fwd = mlstm_chunkwise(q, k, v, i_f, logf_f)
    h_bwd = flip(mlstm_chunkwise(flip(q), flip(k), flip(v), flip(i_b), flip(logf_b)))
    h = (h_fwd + h_bwd).transpose(0, 2, 1, 3)
    h = h * lax.rsqrt(jnp.mean(h * h, axis=-1, keepdims=True) + NORM_EPS)
    h = h * out_norm_g.astype(jnp.float32).reshape(MLSTM_HEADS, MLSTM_HEAD_DIM)
    h = h.reshape(B, S, MLSTM_WIDTH).astype(x_m.dtype) + skip * xc
    return h * jax.nn.sigmoid(o_pre)

def expert_choice_ffn(h, w_router, b_router, w_gate, w_up, w_down):
    B, S, D = h.shape
    cap = (EC_CAPACITY_FACTOR * S) // N_EXPERTS
    logits = (h @ w_router + b_router).astype(jnp.float32)
    affinity = jax.nn.softmax(logits, axis=-1)
    gates, idx = lax.top_k(affinity.transpose(0, 2, 1), cap)
    bidx = jnp.arange(B)[:, None, None]
    xin = h[bidx, idx]
    hid = jax.nn.silu(jnp.einsum('becd,edf->becf', xin, w_gate)) * jnp.einsum('becd,edf->becf', xin, w_up)
    y = jnp.einsum('becf,efd->becd', hid, w_down) * gates[..., None].astype(h.dtype)
    return jnp.zeros_like(h).at[bidx, idx].add(y)

def first_inputs(seed: int = 0) -> dict:
    key = jax.random.key(seed)
    ks = jax.random.split(key, 26)
    f32 = jnp.float32
    nrm = lambda k, shape, scale: scale * jax.random.normal(k, shape, f32)
    L = DEPTH
    H = MLSTM_HEADS
    nblk = MLSTM_WIDTH // MLSTM_QKV_BLOCK
    return {
        "x": nrm(ks[0], (BATCH, SEQ, D_MODEL), 1.0),
        "c": nrm(ks[1], (BATCH, D_MODEL), 1.0),
        "w_ada": nrm(ks[2], (L, D_MODEL, N_MOD * D_MODEL), 0.5 * D_MODEL ** -0.5),
        "b_ada": nrm(ks[3], (L, N_MOD * D_MODEL), 0.02),
        "norm1_g": 1.0 + nrm(ks[4], (L, D_MODEL), 0.02),
        "w_in": nrm(ks[5], (L, D_MODEL, PROJ_TOTAL), D_MODEL ** -0.5),
        "conv_w": nrm(ks[6], (L, MLSTM_CONV, MLSTM_WIDTH), MLSTM_CONV ** -0.5),
        "conv_b": nrm(ks[7], (L, MLSTM_WIDTH), 0.02),
        "w_q_blk": nrm(ks[8], (L, nblk, MLSTM_QKV_BLOCK, MLSTM_QKV_BLOCK), MLSTM_QKV_BLOCK ** -0.5),
        "w_k_blk": nrm(ks[9], (L, nblk, MLSTM_QKV_BLOCK, MLSTM_QKV_BLOCK), MLSTM_QKV_BLOCK ** -0.5),
        "w_v_blk": nrm(ks[10], (L, nblk, MLSTM_QKV_BLOCK, MLSTM_QKV_BLOCK), MLSTM_QKV_BLOCK ** -0.5),
        "b_igate": nrm(ks[11], (L, 2, H), 0.1),
        "b_fgate": jnp.linspace(3.0, 6.0, H, dtype=f32)[None, None, :] + nrm(ks[12], (L, 2, H), 0.1),
        "mlstm_norm_g": 1.0 + nrm(ks[13], (L, MLSTM_WIDTH), 0.02),
        "mlstm_skip": 1.0 + nrm(ks[14], (L, MLSTM_WIDTH), 0.02),
        "q_norm_g": 1.0 + nrm(ks[15], (L, ATTN_HEAD_DIM), 0.02),
        "k_norm_g": 1.0 + nrm(ks[16], (L, ATTN_HEAD_DIM), 0.02),
        "rel_bias": nrm(ks[17], (REL_BUCKETS, ATTN_HEADS), 0.5),
        "w_out": nrm(ks[18], (L, MIX_WIDTH, D_MODEL), MIX_WIDTH ** -0.5),
        "norm2_g": 1.0 + nrm(ks[19], (L, D_MODEL), 0.02),
        "w_router": nrm(ks[20], (L, D_MODEL, N_EXPERTS), D_MODEL ** -0.5),
        "b_router": nrm(ks[21], (L, N_EXPERTS), 0.01),
        "w_gate": nrm(ks[22], (L, N_EXPERTS, D_MODEL, D_FF_EXPERT), D_MODEL ** -0.5),
        "w_up": nrm(ks[23], (L, N_EXPERTS, D_MODEL, D_FF_EXPERT), D_MODEL ** -0.5),
        "w_down": nrm(ks[24], (L, N_EXPERTS, D_FF_EXPERT, D_MODEL), D_FF_EXPERT ** -0.5),
    }

def first_block(x, c, w_ada, b_ada, norm1_g, w_in, conv_w, conv_b, w_q_blk, w_k_blk, w_v_blk,
              b_igate, b_fgate, mlstm_norm_g, mlstm_skip, q_norm_g, k_norm_g, rel_bias, w_out,
              norm2_g, w_router, b_router, w_gate, w_up, w_down):
    split_points = [int(s) for s in np.cumsum(PROJ_WIDTHS)[:-1]]
    for l in range(DEPTH):
        mod = jax.nn.silu(c) @ w_ada[l] + b_ada[l]
        shift1, scale1, gate1, shift2, scale2, gate2 = jnp.split(mod[:, None, :], N_MOD, axis=-1)

        h = rms_norm(x, norm1_g[l]) * (1.0 + scale1) + shift1
        proj = h @ w_in[l]
        x_m, o_pre, i_fw, f_fw, i_bw, f_bw, a_q, a_k, a_v = jnp.split(proj, split_points, axis=-1)
        y_mlstm = mlstm_mixer(x_m, o_pre, i_fw, f_fw, i_bw, f_bw, conv_w[l], conv_b[l], w_q_blk[l],
                              w_k_blk[l], w_v_blk[l], b_igate[l], b_fgate[l], mlstm_norm_g[l], mlstm_skip[l])
        y_attn = dilated_attention_mixer(a_q, a_k, a_v, q_norm_g[l], k_norm_g[l], rel_bias)
        mix = jnp.concatenate([y_mlstm, y_attn], axis=-1) @ w_out[l]
        x = x + gate1 * mix

        h2 = rms_norm(x, norm2_g[l]) * (1.0 + scale2) + shift2
        x = x + gate2 * expert_choice_ffn(h2, w_router[l], b_router[l], w_gate[l], w_up[l], w_down[l])
    return x


DEPTH_2 = 2

N_META = 16
CHUNK = 128
PAD = (-N_META) % CHUNK
RET_HEADS = 4
RET_DK = 48
RET_DV = 96
RET_QK = RET_HEADS * RET_DK
RET_W = RET_HEADS * RET_DV
POOL_WINDOWS = (2, 4, 8, 16)
POOL_GROUP = 64
POOL_W = len(POOL_WINDOWS) * POOL_GROUP
FOX_HEADS = 6
FOX_DH = 64
FOX_W = FOX_HEADS * FOX_DH
D_MIX = RET_W + POOL_W + FOX_W
IN_SPLITS = (RET_QK, RET_QK, RET_W, RET_W, POOL_W, FOX_W, FOX_W, FOX_W, FOX_HEADS)
D_IN = sum(IN_SPLITS)
D_FF = -(-8 * D_MODEL // (3 * 256)) * 256
ROPE_BASE = 10000.0
LN_EPS = 1e-5
NEG_INF = -1e30
ALPHA = (2.0 * DEPTH_2) ** 0.25
BETA = (8.0 * DEPTH_2) ** -0.25


def layer_norm(x, g, b):
    xf = x.astype(jnp.float32)
    mu = jnp.mean(xf, axis=-1, keepdims=True)
    var = jnp.mean(jnp.square(xf - mu), axis=-1, keepdims=True)
    y = (xf - mu) * lax.rsqrt(var + LN_EPS)
    return (y * g + b).astype(x.dtype)

def pad_front(a):
    widths = [(0, 0), (PAD, 0)] + [(0, 0)] * (a.ndim - 2)
    return jnp.pad(a, widths)

def rotary(x, cos, sin):
    half = x.shape[-1] // 2
    x1, x2 = x[..., :half], x[..., half:]
    return jnp.concatenate([x1 * cos - x2 * sin, x1 * sin + x2 * cos], axis=-1)

def retention_chunkwise(q, k, v):
    Bsz, Lp, H, dk = q.shape
    dv = v.shape[-1]
    n = Lp // CHUNK
    gamma = 1.0 - 2.0 ** (-5.0 - jnp.arange(H, dtype=jnp.float32))
    lg = jnp.log(gamma)
    i = jnp.arange(CHUNK, dtype=jnp.float32)
    diff = i[:, None] - i[None, :]
    dmask = jnp.where(diff >= 0, jnp.exp(lg[:, None, None] * jnp.maximum(diff, 0.0)), 0.0)
    xi = jnp.exp(lg[:, None] * (i + 1.0))
    zeta = jnp.exp(lg[:, None] * (CHUNK - 1.0 - i))
    chunk_decay = jnp.exp(lg * CHUNK)
    qc = q.astype(jnp.float32).reshape(Bsz, n, CHUNK, H, dk)
    kc = k.astype(jnp.float32).reshape(Bsz, n, CHUNK, H, dk) * (dk ** -0.5)
    vc = v.astype(jnp.float32).reshape(Bsz, n, CHUNK, H, dv)
    scores = jnp.einsum('bnihd,bnjhd->bnhij', qc, kc) * dmask
    inner = jnp.einsum('bnhij,bnjhe->bnihe', scores, vc)
    kv = jnp.einsum('bnjhd,hj,bnjhe->nbhde', kc, zeta, vc)

    def step(state, kv_n):
        return state * chunk_decay[None, :, None, None] + kv_n, state

    _, prev = lax.scan(step, jnp.zeros_like(kv[0]), kv)
    cross = jnp.einsum('bnihd,nbhde,hi->bnihe', qc, prev, xi)
    return (inner + cross).reshape(Bsz, Lp, H, dv)

def multiscale_pool(u, pool_w, pool_scale):
    Bsz, L, _ = u.shape
    G = len(POOL_WINDOWS)
    uf = u.astype(jnp.float32).reshape(Bsz, L, G, POOL_GROUP)
    cs = jnp.concatenate([jnp.zeros((Bsz, 1, G, POOL_GROUP), jnp.float32),
                          jnp.cumsum(uf, axis=1)], axis=1)
    t = jnp.arange(L)
    outs = []
    for g, w in enumerate(POOL_WINDOWS):
        lo = jnp.maximum(t + 1 - w, 0)
        cnt = (t + 1 - lo).astype(jnp.float32)
        window_sum = cs[:, t + 1, g] - cs[:, lo, g]
        outs.append(window_sum / cnt[None, :, None] - uf[:, :, g])
    pooled = jnp.stack(outs, axis=2)
    y = jnp.einsum('blgc,gcd->blgd', pooled, pool_w.astype(jnp.float32)).reshape(Bsz, L, POOL_W)
    return y * pool_scale

def forgetting_attention(q, k, v, logf):
    Bsz, Lp, H, d = q.shape
    c = jnp.cumsum(logf.astype(jnp.float32), axis=1).transpose(0, 2, 1)
    qf = q.astype(jnp.float32) * (d ** -0.5)
    kf = k.astype(jnp.float32)
    vf = v.astype(jnp.float32)
    kpos = jnp.arange(Lp)
    key_ok = kpos >= PAD
    nb = Lp // CHUNK

    def block(ib):
        start = ib * CHUNK
        qb = lax.dynamic_slice_in_dim(qf, start, CHUNK, axis=1)
        cb = lax.dynamic_slice_in_dim(c, start, CHUNK, axis=2)
        qpos = start + jnp.arange(CHUNK)
        s = jnp.einsum('bihd,bjhd->bhij', qb, kf)
        s = s + cb[..., :, None] - c[..., None, :]
        mask = (kpos[None, :] <= qpos[:, None]) & key_ok[None, :]
        s = jnp.where(mask, s, NEG_INF)
        p = jax.nn.softmax(s, axis=-1)
        return jnp.einsum('bhij,bjhd->bihd', p, vf)

    out = lax.map(block, jnp.arange(nb))
    return out.transpose(1, 0, 2, 3, 4).reshape(Bsz, Lp, H, d)

def head_group_norm(o, g):
    of = o.astype(jnp.float32)
    mu = jnp.mean(of, axis=-1, keepdims=True)
    var = jnp.mean(jnp.square(of - mu), axis=-1, keepdims=True)
    y = ((of - mu) * lax.rsqrt(var + LN_EPS)).reshape(o.shape[0], o.shape[1], -1)
    return y * g

def hybrid_layer(h, w_in, b_f, ret_gn_g, pool_w, pool_scale, w_out,
                 ln1_g, ln1_b, w1, w3, w2, ln2_g, ln2_b, cos, sin):
    Bsz, L, _ = h.shape
    proj = jnp.einsum('bld,de->ble', h, w_in)
    parts = []
    off = 0
    for sz in IN_SPLITS:
        parts.append(proj[..., off:off + sz])
        off += sz
    q_r, k_r, v_r, g_r, u_p, q_f, k_f, v_f, f_logit = parts

    qr = rotary(pad_front(q_r.reshape(Bsz, L, RET_HEADS, RET_DK)), cos, sin)
    kr = rotary(pad_front(k_r.reshape(Bsz, L, RET_HEADS, RET_DK)), cos, sin)
    vr = pad_front(v_r.reshape(Bsz, L, RET_HEADS, RET_DV))
    o_r = retention_chunkwise(qr, kr, vr)[:, PAD:]
    o_r = jax.nn.silu(g_r.astype(jnp.float32)) * head_group_norm(o_r, ret_gn_g)

    o_p = multiscale_pool(u_p, pool_w, pool_scale)

    logf = jax.nn.log_sigmoid(f_logit.astype(jnp.float32) + b_f)
    o_f = forgetting_attention(pad_front(q_f.reshape(Bsz, L, FOX_HEADS, FOX_DH)),
                               pad_front(k_f.reshape(Bsz, L, FOX_HEADS, FOX_DH)),
                               pad_front(v_f.reshape(Bsz, L, FOX_HEADS, FOX_DH)),
                               pad_front(logf))[:, PAD:].reshape(Bsz, L, FOX_W)

    mix = jnp.concatenate([o_r, o_p, o_f], axis=-1)
    mix = jnp.einsum('ble,ed->bld', mix, w_out)
    h = layer_norm(ALPHA * h + mix, ln1_g, ln1_b)

    a = jnp.einsum('bld,df->blf', h, w1)
    b = jnp.einsum('bld,df->blf', h, w3)
    y = jnp.einsum('blf,fd->bld', jax.nn.silu(a) * b, w2)
    return layer_norm(ALPHA * h + y, ln2_g, ln2_b)

def second_inputs(seed: int = 0) -> dict:
    key = jax.random.key(seed)
    ks = jax.random.split(key, 20)
    f32 = jnp.float32
    x = jax.random.normal(ks[0], (BATCH, SEQ, D_MODEL), f32)
    meta = jax.random.normal(ks[1], (N_META, D_MODEL), f32)
    ln_emb_g = 1.0 + 0.01 * jax.random.normal(ks[2], (D_MODEL,), f32)
    ln_emb_b = 0.01 * jax.random.normal(ks[3], (D_MODEL,), f32)
    w_in = jax.random.normal(ks[4], (DEPTH_2, D_MODEL, D_IN), f32) * D_MODEL ** -0.5
    b_f = jax.random.uniform(ks[5], (DEPTH_2, FOX_HEADS), f32, 1.0, 4.0)
    ret_gn_g = 1.0 + 0.01 * jax.random.normal(ks[6], (DEPTH_2, RET_W), f32)
    pool_w = jax.random.normal(ks[7], (DEPTH_2, len(POOL_WINDOWS), POOL_GROUP, POOL_GROUP), f32) * POOL_GROUP ** -0.5
    pool_scale = 1.0 + 0.1 * jax.random.normal(ks[8], (DEPTH_2, POOL_W), f32)
    w_out = jax.random.normal(ks[9], (DEPTH_2, D_MIX, D_MODEL), f32) * (D_MIX ** -0.5) * BETA
    ln1_g = 1.0 + 0.01 * jax.random.normal(ks[10], (DEPTH_2, D_MODEL), f32)
    ln1_b = 0.01 * jax.random.normal(ks[11], (DEPTH_2, D_MODEL), f32)
    w_ffn1 = jax.random.normal(ks[12], (DEPTH_2, D_MODEL, D_FF), f32) * D_MODEL ** -0.5
    w_ffn3 = jax.random.normal(ks[13], (DEPTH_2, D_MODEL, D_FF), f32) * D_MODEL ** -0.5
    w_ffn2 = jax.random.normal(ks[14], (DEPTH_2, D_FF, D_MODEL), f32) * (D_FF ** -0.5) * BETA
    ln2_g = 1.0 + 0.01 * jax.random.normal(ks[15], (DEPTH_2, D_MODEL), f32)
    ln2_b = 0.01 * jax.random.normal(ks[16], (DEPTH_2, D_MODEL), f32)
    return {'x': x, 'meta': meta, 'ln_emb_g': ln_emb_g, 'ln_emb_b': ln_emb_b,
            'w_in': w_in, 'b_f': b_f, 'ret_gn_g': ret_gn_g, 'pool_w': pool_w,
            'pool_scale': pool_scale, 'w_out': w_out, 'ln1_g': ln1_g, 'ln1_b': ln1_b,
            'w_ffn1': w_ffn1, 'w_ffn3': w_ffn3, 'w_ffn2': w_ffn2,
            'ln2_g': ln2_g, 'ln2_b': ln2_b}

def second_block(x, meta, ln_emb_g, ln_emb_b, w_in, b_f, ret_gn_g, pool_w, pool_scale,
              w_out, ln1_g, ln1_b, w_ffn1, w_ffn3, w_ffn2, ln2_g, ln2_b):
    Bsz = x.shape[0]
    h = jnp.concatenate([jnp.broadcast_to(meta[None].astype(x.dtype), (Bsz, N_META, D_MODEL)), x], axis=1)
    h = layer_norm(h, ln_emb_g, ln_emb_b)
    L = h.shape[1]
    Lp = L + PAD
    pos = jnp.arange(Lp, dtype=jnp.float32) - PAD
    inv_freq = ROPE_BASE ** (-jnp.arange(RET_DK // 2, dtype=jnp.float32) / (RET_DK // 2))
    ang = pos[:, None] * inv_freq[None, :]
    cos = jnp.cos(ang)[:, None, :]
    sin = jnp.sin(ang)[:, None, :]
    for l in range(DEPTH_2):
        h = hybrid_layer(h, w_in[l], b_f[l], ret_gn_g[l], pool_w[l], pool_scale[l], w_out[l],
                         ln1_g[l], ln1_b[l], w_ffn1[l], w_ffn3[l], w_ffn2[l], ln2_g[l], ln2_b[l],
                         cos, sin)
    return h[:, N_META:]


def setup_inputs(seed=0):
    out = dict(first_inputs(seed))
    for name, value in second_inputs(seed + 1).items():
        if name != "x":
            out[name + "_2"] = value
    return out


def reference(
    x, c, w_ada, b_ada, norm1_g, w_in, conv_w, conv_b, w_q_blk, w_k_blk, w_v_blk, b_igate,
    b_fgate, mlstm_norm_g, mlstm_skip, q_norm_g, k_norm_g, rel_bias, w_out, norm2_g, w_router,
    b_router, w_gate, w_up, w_down, meta_2, ln_emb_g_2, ln_emb_b_2, w_in_2, b_f_2, ret_gn_g_2,
    pool_w_2, pool_scale_2, w_out_2, ln1_g_2, ln1_b_2, w_ffn1_2, w_ffn3_2, w_ffn2_2, ln2_g_2,
    ln2_b_2,
):
    x = first_block(
        x, c, w_ada, b_ada, norm1_g, w_in, conv_w, conv_b, w_q_blk, w_k_blk, w_v_blk, b_igate,
        b_fgate, mlstm_norm_g, mlstm_skip, q_norm_g, k_norm_g, rel_bias, w_out, norm2_g,
        w_router, b_router, w_gate, w_up, w_down,
    )
    return second_block(
        x, meta_2, ln_emb_g_2, ln_emb_b_2, w_in_2, b_f_2, ret_gn_g_2, pool_w_2, pool_scale_2,
        w_out_2, ln1_g_2, ln1_b_2, w_ffn1_2, w_ffn3_2, w_ffn2_2, ln2_g_2, ln2_b_2,
    )


_drawn_inputs = setup_inputs


def setup_inputs(seed=0):
    import zlib

    import numpy as np

    out = dict(_drawn_inputs(seed))
    spreads = {}
    factors = {'b_ada': 2.781,
     'norm1_g': 7.167,
     'conv_b': 5.921,
     'b_igate': 8.0,
     'mlstm_norm_g': 8.0,
     'mlstm_skip': 8.0,
     'q_norm_g': 8.0,
     'k_norm_g': 8.0,
     'rel_bias': 4.047,
     'norm2_g': 7.776,
     'b_router': 8.0,
     'ln_emb_g_2': 5.21,
     'ln_emb_b_2': 5.007,
     'ret_gn_g_2': 8.0,
     'ln1_g_2': 3.84,
     'ln1_b_2': 3.758,
     'ln2_g_2': 4.111,
     'ln2_b_2': 3.891}
    for name, (base, spread) in spreads.items():
        noise = np.random.default_rng([zlib.crc32(name.encode()), seed]).standard_normal(out[name].shape)
        drawn = base * np.exp(spread * noise) if base else spread * noise
        out[name] = jnp.asarray(drawn.astype(out[name].dtype))
    for name, factor in factors.items():
        out[name] = (out[name] * factor).astype(out[name].dtype)
    return out
```

```python
import math
from contextlib import ExitStack

import numpy as np

import concourse.bass as bass
from concourse import mybir

F32 = mybir.dt.float32
FR = mybir.dt.float32r
ALU = mybir.AluOpType
ACT = mybir.ActivationFunctionType
AX_X = mybir.AxisListType.X

P = 128
S = 512
D = 1024
KC = D // P
TT = S // P
SLOT = 4096
NSLOT = 6
MH, MD = 4, 128
AH, AD = 8, 64
TAPS = 5
NE, CAP, DFE = 16, 64, 2048
EPS1 = 1e-6

ROW_ADA, ROW_N1, ROW_C, ROW_N2, ROW_CW, ROW_CB, ROW_MG, ROW_SK, ROW_QG, ROW_KG = 0, 48, 56, 64, 72, 92, 96, 100, 104, 105
FIRST = 64
ROWS_A = 106
GROUP = 37
ROWS_B = 16 + 2 * GROUP
DIFFS = 2 * S - 1


ARENA = 24800

META = 16
L2 = S + META
LAYERS = 2
RH, RK, RV = 4, 48, 96
FH, FD = 6, 64
DFF = 2816
FC = DFF // P
GROUPS_W = (2, 4, 8, 16)
PADW = max(GROUPS_W)
EPS2 = 1e-5
ALPHA = (2.0 * LAYERS) ** 0.25
NEG = -1e30
LAYER_UNITS, SLOT2, NSLOT2 = 36, 6144, 4


class Plan:

    def __init__(self, stages, base=0):
        self.first, self.size, self.base, self.total = {}, {}, base, 0
        self.start = base
        for name, n in stages:
            assert name not in self.first
            self.first[name], self.size[name] = self.total, n
            self.total += n

    def layer(self, l):
        p = Plan([], self.base)
        p.first, p.size, p.total = self.first, self.size, self.total
        p.start = l * self.total + self.base
        return p

    def count(self, stage, i=None):
        return self.start + (self.first[stage] + (self.size[stage] if i is None else i + 1))

    def claim(self, pe, banks, freed, stage, i):
        n = self.first[stage] + i
        if self.base or n >= len(banks):
            pe.wait_ge(freed, self.start + (n + 1 - len(banks)))
        return banks[n % len(banks)]

    def take(self, eng, banks, filled, stage, i):
        n = self.first[stage] + i
        eng.wait_ge(filled, self.start + (n + 1))
        return banks[n % len(banks)]


def program(nc, a, out):
    with ExitStack() as ctx:
        def sb(name, shape):
            return ctx.enter_context(nc.sbuf_tensor(name, shape, F32))

        def sem(name):
            return ctx.enter_context(nc.semaphore(name))

        vpsum = ctx.enter_context(nc.psum_tensor("vpsum", [P, 4, 512], F32))
        apsum = ctx.enter_context(nc.psum_tensor("apsum", [P, 4, 512], F32))
        vbank = [vpsum[:, i, :] for i in range(4)]
        abank = [apsum[:, i, :] for i in range(4)]

        with ExitStack() as names:
            ring = names.enter_context(nc.sbuf_tensor("ring", [P, NSLOT, SLOT], F32))
            arena = names.enter_context(nc.sbuf_tensor("arena", [P, ARENA], F32))
        ring_r = sb("ring_r", [P, NSLOT, SLOT])
        arena_r = sb("arena_r", [P, ARENA])

        def region(start, n, pattern, **kw):
            return arena[:, start:start + n].rearrange(pattern, **kw)

        R0 = 0
        xtok = region(R0, TT * D, "p (t d) -> p t d", t=TT)
        hT = region(R0, KC * S, "p (c t) -> p c t", c=KC)
        asq = region(R0, 8 * S, "p (c t) -> p c t", c=8)
        yT = region(R0, KC * S, "p (c t) -> p c t", c=KC)
        R1 = R0 + 4096
        xm = region(R1, MH * (S + 4), "p (c t) -> p c t", c=MH)
        htok = region(R1, TT * S, "p (t c) -> p t c", t=TT)
        R2 = R1 + MH * (S + 4)
        sigo = region(R2, MH * S, "p (c t) -> p c t", c=MH)
        R3 = R2 + MH * S
        xT = region(R3, KC * S, "p (c t) -> p c t", c=KC)
        sq = region(R3 + 4096, KC * S, "p (c t) -> p c t", c=KC)
        aq = region(R3, 4 * S, "p (c t) -> p c t", c=4)
        ak = region(R3 + 2048, 4 * S, "p (c t) -> p c t", c=4)
        av = region(R3 + 4096, 4 * S, "p (t c) -> p t c", t=TT)
        atok = region(R3 + 6144, TT * S, "p (t c) -> p t c", t=TT)
        R4 = R3 + 8192
        toep = region(R4, 2 * 896, "p (a x) -> p a x", a=2)
        qz = region(R4 + 1792, 2 * S, "p (a x) -> p a x", a=2)
        logit = region(R4 + 2816, 2 * S, "p (a x) -> p a x", a=2)
        prob = region(R4 + 3840, 2 * S, "p (a x) -> p a x", a=2)
        probT = region(R4 + 4864, 2 * S, "p (a x) -> p a x", a=2)
        gates = region(R4 + 2816, 5 * S, "p (k t) -> p k t", k=5)
        R5 = R4 + 5888
        hankel = region(R5, 1024, "p (a x) -> p a x", a=1)
        modr = region(R5, 1024, "p (a x) -> p a x", a=2)
        xc = region(R3, MH * S, "p (c t) -> p c t", c=MH)
        qm = region(R3 + 2048, MH * S, "p (c t) -> p c t", c=MH)
        km = region(R3 + 4096, MH * S, "p (c t) -> p c t", c=MH)
        vm = region(R3 + 6144, TT * MH * 129, "p (t h d) -> p t h d", t=TT, h=MH)
        wbd = region(R3 + 8208, 3 * MH * P, "p (i h d) -> p i h d", i=3, h=MH)
        W = region(R3 + 9744, 2 * 1280, "p (d x) -> p d x", d=2)
        E = region(R3 + 12304, 2 * 2 * S, "p (a d t) -> p a d t", a=2, d=2)
        assert R3 + 14352 <= R5 + 1024 <= ARENA

        def Wt(d, jt):
            start, width = (sum(S - P * j for j in range(jt)), S - P * jt) if d == 0 else \
                           (sum(P * (j + 1) for j in range(jt)), P * (jt + 1))
            return W[:, d, start:start + width]

        shared = sb("shared", [P, 2176])

        def share(start, n, pattern=None, rows=P, **kw):
            part = shared[0:rows, start:start + n]
            return part.rearrange(pattern, **kw) if pattern else part

        head_ones, flip = share(0, P), share(128, P)
        rowsA, rowsB = share(256, P, rows=ROWS_A), share(384, P, rows=ROWS_B)
        cs32 = share(512, KC * 32, "p (c o) -> p c o", c=KC)
        wgate = share(768, KC * 80, "p (c k m) -> p c k m", c=KC, k=2)
        gcol = share(1408, 320, "p (k r) -> p k r", r=40)
        gneg = share(1728, 160, "p (k r) -> p k r", r=40)
        wrout = share(1888, KC * NE, "p (c e) -> p c e", e=NE)
        mu, rstd = share(0, L2), share(528, L2)
        negc = share(1056, L2, rows=FH)
        pwL = share(1584, 2 * P, "p (c d) -> p c d", c=2)
        rotm, tri = share(1840, P), share(1968, P)
        metar = sb("metar", [P, P])
        rms1 = arena[:, 23312:23824]
        negM = arena[0:40, 23824:24336]
        ident = sb("ident", [P, P])
        ones = sb("ones", [P, P])
        colsA = sb("colsA", [P, ROWS_A])
        colsB = sb("colsB", [P, ROWS_B])
        cs = sb("cs", [P, KC])
        inv32 = sb("inv32", [P, 1])
        eps1 = sb("eps1", [P, 1])
        mod = sb("mod", [P, 48])
        g1s = sb("g1s", [P, KC])
        bgate = sb("bgate", [40, 2])
        wraw = sb("wraw", [P, 3, MH, 4])
        bmask = sb("bmask", [P, 32])
        qg8 = sb("qg8", [P, 1])
        ast = sb("ast", [P, 4, 4])
        hst = sb("hst", [P, 3, 16])
        den = sb("den", [P, 2])
        bvec_d = nc.dram_tensor("bvec_d", (AH, DIFFS), F32, kind="Internal").ap()
        x_d = nc.dram_tensor("x_d", (P, KC * S), F32, kind="Internal").ap()
        btab = arena[0:33, R3 + 6144 + 1024:R3 + 6144 + 1024 + DIFFS]
        bvec = arena[0:AH, R3 + 6144 + 0:R3 + 6144 + DIFFS]
        bval = sb("bval", [33, AH])

        def mod_stages(lo, hi):
            return [st for i in range(lo, hi) for st in [(f"modrow{i}", 1), (f"modcol{i}", 1)]]

        def attention_stages():
            for u in range(AU + 2):
                if u < AU:
                    if u % TT == 0:
                        yield f"toep{u // TT}", 2
                    yield f"logits{u}", 1
                if u >= 2:
                    yield f"aout{u - 2}", 1

        AU = AH * TT
        V = Plan([("xT", KC), ("colsA", 1)] + mod_stages(0, 4) + [("xm", MH), ("qk", 8), ("gates", 2), ("colsA2", 1), ("colsB", 1)]
                 + mod_stages(4, 12) + [("bvec", 3), ("gcol", 1)] + list(attention_stages())
                 + [("vm", TT)] + [st for h in range(MH) for st in [(f"score{h}", TT), (f"hout{h}", 2 * TT)]]
                 + [("ymT", MH), ("mix", KC), ("route", 1), ("affE", 1), ("rankE", 1)])
        A = Plan([("ms1p", 1), ("ms1", 1), ("sigo", MH), ("av", TT), ("ss", 8), ("probT", AU), ("yaT", 4),
                  ("qkm", 2 * MH)] + [(f"rows{h}", 2) for h in range(MH)] + [("ms2p", 1), ("ms2", 1), ("h2tok", 2 * TT)])

        v_filled, v_freed = sem("v_filled"), sem("v_freed")
        a_filled, a_freed = sem("a_filled"), sem("a_freed")
        loaded = [sem(f"loaded{i}") for i in range(NSLOT)]
        vecA_in, vecB_in, x_in, gate_in, wraw_in, bias_in = sem("vecA_in"), sem("vecB_in"), sem("x_in"), sem("gate_in"), sem("wraw_in"), sem("bias_in")
        pool_const, dve_const = sem("pool_const"), sem("dve_const")
        dve_step, act_step = sem("dve_step"), sem("act_step")
        silu_c, cs_ready, sq_done, h_done, x_stored = sem("silu_c"), sem("cs_ready"), sem("sq_done"), sem("h_done"), sem("x_stored")
        conv_done, xc_done, wbd_done = sem("conv_done"), sem("xc_done"), sem("wbd_done")
        logf_part, m_done, expm_done = sem("logf_part"), sem("m_done"), sem("expm_done")
        asq_done, qk_normed, gneg_done = sem("asq_done"), sem("qk_normed"), sem("gneg_done")
        bvec_out, hankel_in = sem("bvec_out"), sem("hankel_in")
        qz_done, logits_done, prob_done = sem("qz_done"), sem("logits_done"), sem("prob_done")
        factor_done, factor_cut, weight_done = sem("factor_done"), sem("factor_cut"), sem("weight_done")
        hsq_done, hrms_done, hnorm_done, ym_done = sem("hsq_done"), sem("hrms_done"), sem("hnorm_done"), sem("ym_done")
        out_sem = sem("out_sem")

        w_in = a["w_in"][0].rearrange("(c p) n -> p c n", p=P)
        w_ada = a["w_ada"][0].rearrange("(c p) n -> p c n", p=P)
        w_out = a["w_out"][0].rearrange("(c p) n -> p c n", p=P)
        ADA, XM_U, O_U, Q_U, K_U, V_U, ADA2, OUT_U = 0, 4, 5, 6, 7, 8, 9, 17
        units = [(w_ada[:, :, 512 * i:512 * i + 512], v_filled, V.count(f"modrow{i}")) for i in range(4)]
        units += [(w_in[:, :, 0:512], v_filled, V.count("xm")), (w_in[:, :, 512:1024], a_filled, A.count("sigo")),
                  (w_in[:, :, 1040:1552], v_filled, V.count("qk", 3)), (w_in[:, :, 1552:2064], v_filled, V.count("qk", 7)),
                  (w_in[:, :, 2064:2576], a_filled, A.count("av"))]
        units += [(w_ada[:, :, 512 * i:512 * i + 512], v_filled, V.count(f"modrow{i}")) for i in range(4, 12)]
        units += [(w_out[:, :, 512 * i:512 * i + 512], v_filled, V.count("mix", 4 * i + 3)) for i in range(2)]

        def slot(n):
            return ring[:, n % NSLOT, :].rearrange("p (c n) -> p c n", c=KC)


        x2 = region(4096, KC * S, "p (c t) -> p c t", c=KC)
        xre = region(8192, KC * S, "p (c t) -> p c t", c=KC)
        h2tok = region(8192, TT * D, "p (t d) -> p t d", t=TT)
        sq2 = region(12288, KC * S, "p (c t) -> p c t", c=KC)
        h2T = region(R0, KC * S, "p (c t) -> p c t", c=KC)
        acc = region(R0, KC * S, "p (c t) -> p c t", c=KC)
        M0 = 12288
        aff = arena[0:NE, M0:M0 + S]
        work = arena[0:NE, M0 + 512:M0 + 1024]
        picked = arena[0:NE, M0 + 1024:M0 + 1536]
        rank = arena[0:NE, M0 + 1536:M0 + 2048]
        top8 = arena[0:NE, M0 + 2048:M0 + 2056]
        sel = region(M0 + 2560, TT * 2 * CAP, "p (t a c) -> p t a c", t=TT, a=2)
        selg = region(M0 + 3072, TT * 2 * CAP, "p (t a c) -> p t a c", t=TT, a=2)
        selT = region(M0 + 3584, S, "p (a t) -> p a t", a=1)
        xin = region(M0 + 4096, KC * CAP, "p (c n) -> p c n", c=KC)
        sg = region(M0 + 4608, 2 * 512, "p (g f) -> p g f", g=2)
        hid = region(M0 + 5632, 2 * 512, "p (g f) -> p g f", g=2)
        hidT = region(M0 + 6656, 2 * 512, "p (g j n) -> p g j n", g=2, j=4)
        ysb = region(M0 + 7680, D, "p (a d) -> p a d", a=1)
        slots_iota = region(M0 + 8704, TT * 2 * CAP, "p (t a c) -> p t a c", t=TT, a=2)
        assert M0 + 9216 <= ARENA

        brout = sb("brout", [1, NE])
        g2s = sb("g2s", [P, KC])
        rst = sb("rst", [P, 3, TT])
        rlog = sb("rlog", [P, TT, NE])
        affT = sb("affT", [P, TT, NE + 1])
        rankT = sb("rankT", [P, TT, NE + 1])

        rout_in, xre_in, sq2_done, h2_done = sem("rout_in"), sem("xre_in"), sem("sq2_done"), sem("h2_done")
        rexp_ready, rexp_done, aff_done, rank_done = sem("rexp_ready"), sem("rexp_done"), sem("aff_done"), sem("rank_done")
        iota_done = sem("iota_done")
        gu_done = sem("gu_done")
        down_done = sem("down_done")
        hT_done = sem("hT_done")
        gather_done = sem("gather_done")
        selT_done = sem("selT_done")
        scatter_done = sem("scatter_done")
        silu_done = sem("silu_done")
        hT_copied = sem("hT_copied")
        xin_copied = sem("xin_copied")
        selT_copied = sem("selT_copied")
        y_copied = sem("y_copied")
        hid_done = sem("hid_done")
        sel_done = sem("sel_done")
        acc_done = sem("acc_done")
        x3_done = sem("x3_done")
        G_BANK, U_BANK = (vbank[0], vbank[2]), (vbank[1], vbank[3])
        Y_BANK = (vbank[0], vbank[1])
        HT_BANK = (abank[0], abank[1])
        XIN_BANK, SELT_BANK = abank[2], abank[3]
        OUT_BANK = (vbank[2], vbank[3], abank[0], abank[1])
        MOE_U = len(units)
        EXPERT = D * DFE

        def expert_unit(sp, e, j):
            what, g = (("w_gate", 0), ("w_up", 0), ("w_gate", 1), ("w_up", 1), ("w_down", 0), ("w_down", 1))[j // 2]
            r = j % 2
            start, row = ((1024 * g + 512 * r) * D, D) if what == "w_down" else (512 * r * DFE + 1024 * g, DFE)
            offset = e * EXPERT + start
            if not isinstance(e, int):
                sp.lower_val(offset * 4)
            return bass.AP(a[what].tensor, offset, [[row, P], [P * row, 4], [1, 1024]])

        def expert_slot(j):
            return ring[:, (MOE_U + j) % NSLOT, :].rearrange("p (c n) -> p c n", c=4)

        def expert_loaded(e, j):
            return 16 * ((MOE_U + j) // NSLOT + 1) + 32 * e

        def rows528(start, n):
            return region(start, n * L2, "p (c t) -> p c t", c=n)

        H = rows528(0, KC)
        X = rows528(4224, KC)
        xsq = rows528(8448, KC)
        X0, x0sq = rows528(8448, KC), rows528(12672, KC)
        hidden = rows528(8448, FC)
        mixT = rows528(17120, KC)
        S0 = 4224
        raw = rows528(S0, 2)
        rtmp = rows528(S0 + 1056, 1)
        qzr = rows528(S0 + 1584, RH)
        kr = rows528(S0 + 3696, 2)
        vr = region(S0 + 4752, 5 * RH * RV, "p (t c) -> p t c", t=5)
        retW = arena[:, S0 + 6672:S0 + 8480]
        otok = region(S0 + 8480, 5 * RH * RV, "p (t c) -> p t c", t=5)
        sgr = rows528(S0 + 10400, 3)
        qf = rows528(S0, 3)
        kf = rows528(S0 + 1584, 3)
        vf = region(S0 + 3168, 5 * FH * FD, "p (t c) -> p t c", t=5)
        upad = region(S0 + 5088, 2 * (PADW + L2), "p (c x) -> p c x", c=2)
        sumA = region(S0 + 6176, 2 * (PADW + L2), "p (c x) -> p c x", c=2)
        sumB = arena[:, S0 + 7264:S0 + 7808]
        flin = arena[0:FH, S0 + 7808:S0 + 8336]
        fln = arena[0:FH, S0 + 11984:S0 + 12512]
        qzf = rows528(S0 + 5088, 2)
        cb = rows528(S0 + 6144, 2)
        flog = rows528(S0 + 7200, 3)
        fpT = region(S0 + 8784, 2 * 640, "p (a x) -> p a x", a=2)
        ftok = region(S0 + 10064, 5 * FH * FD, "p (t c) -> p t c", t=5)
        C0 = ARENA - 3168
        decay = rows528(C0, RH)
        cosT, sinT = arena[:, C0 + 2112:C0 + 2640], arena[:, C0 + 2640:C0 + 3168]
        assert S0 + 12896 == 17120 and C0 >= 17120 + 4224 and C0 >= M0 + 9216
        otile = region(4224, TT * D, "p (a d) -> p a d", a=TT)

        colsL = sb("colsL", [P, GROUP])
        GN, PS, LN1G, LN1B, LN2G, LN2B = 0, 3, 5, 13, 21, 29
        winv = sb("winv", [P, 2])
        wcorr = sb("wcorr", [P, 2, PADW])
        bfc = sb("bfc", [FH, 2])
        gst = sb("gst", [P, 4, 20])
        eps2 = sb("eps2", [P, 1])

        vpair = [vpsum[:, 2 * i:2 * i + 2, :] for i in range(2)]
        apair = [apsum[:, 2 * i:2 * i + 2, :] for i in range(2)]

        def flat(b):
            return b.rearrange("p a x -> p (a x)")

        def halves(x):
            return x.rearrange("p (a x) -> p a x", a=2)

        HW = L2 // 2
        FU = FH * 5

        def fox_v():
            for u in range(FU + 3):
                if u < FU:
                    yield f"fs{u}", 1
                if u >= 3:
                    yield f"fo{u - 3}", 1

        def fox_a():
            for u in range(FU + 2):
                if u < FU and u % 5 == 0:
                    yield f"cb{u // 5}", 1
                if u >= 2:
                    yield f"fp{u - 2}", 1

        VE = Plan([("meta", 1)], base=V.count("rankE"))
        AE = Plan([("sump", 1), ("sum", 1), ("varp", 1), ("var", 1)], base=A.count("h2tok"))
        VL = Plan([("rot", 4)] + [(f"rs{h}", 5) for h in range(RH)] + [("f", 1), ("qf", 3), ("vfm", 1), ("rt", 3)]
                  + list(fox_v()) + [("op", KC), ("fu", FC), ("dn", KC)], base=VE.count("meta"))
        AL = Plan([("raw", 4), ("vr", 5), ] + [st for h in range(RH) for st in [(f"gr{h}", 1), (f"ro{h}", 1)] if st[0] != f"gr{RH - 1}"]
                  + [("u", 2), ("kf", 3), ("vf", 4), ("pm", 2)] + list(fox_a()) + [("ft", 3), ("sum0p", 1), ("sum0", 1), ("var0p", 1), ("var0", 1), ("fg", FC),
                     ("sum1p", 1), ("sum1", 1), ("var1p", 1), ("var1", 1)], base=AE.count("var"))
        assert VL.total % 2 == 0 and AL.total % 2 == 0
        VF = Plan([("out", 2 * TT)], base=VL.layer(LAYERS).start)

        D_IN2 = a["w_in_2"].shape[2]
        UNITS = [[("w_in_2", col, n)] for col, n in ((0, 768), (768, 640), (2560, 6), (1408, 384), (1792, 384), (2176, 384))]
        USED = [(AL, "vr", 4), (AL, "u", 1), (VL, "f", 0), (VL, "qf", 2), (AL, "kf", 2), (VL, "vfm", 0)]
        for i in range(4):
            UNITS.append([("w_out_2", 256 * i, 256)])
            USED.append((VL, "op", 2 * i + 1))
        FFN_U = len(UNITS)
        for i in range(FC):
            UNITS.append([("w_ffn1_2", P * i, P), ("w_ffn3_2", P * i, P)])
            USED.append((VL, "fu", i))
        DOWN_U = len(UNITS)
        for i in range(4):
            UNITS.append([("w_ffn2_2", 256 * i, 256)])
            USED.append((VL, "dn", 2 * i + 1))
        assert len(UNITS) == LAYER_UNITS and LAYER_UNITS % NSLOT2 == 0
        ring2, ring2_r = ring[:].rearrange("p a x -> p (a x)"), ring_r[:].rearrange("p a x -> p (a x)")

        def slot2(n, chunks, parts, cols):
            s0 = (n + 1) % NSLOT2 * SLOT2
            return ring2[:, s0:s0 + chunks * parts * cols].rearrange("p (c k n) -> p c k n", c=chunks, k=parts)

        h_hi, h_lo = (arena_r[:, s:s + KC * L2].rearrange("p (c t) -> p c t", c=KC) for s in (4224, 0))
        WPART = 2 * KC * P

        def weight_part(n, high, ring_=ring2_r):
            s0 = (FFN_U + n + 1) % NSLOT2 * SLOT2 + WPART * high
            return ring_[:, s0:s0 + WPART]

        def slot2_count(n):
            return sum(len(UNITS[m]) for m in range(n + 1) if (m - n) % NSLOT2 == 0)

        SLOT_LOADS = [slot2_count(LAYER_UNITS - NSLOT2 + i) for i in range(NSLOT2)]
        loaded2 = [sem(f"loaded2_{i}") for i in range(NSLOT2)]
        const2_in, meta_in, pw_in, pw_zero, par_done = sem("const2_in"), sem("meta_in"), sem("pw_in"), sem("pw_zero"), sem("par_done")
        centered, sqx_done, scaled, normed = sem("centered"), sem("sqx_done"), sem("scaled"), sem("normed")
        rot_done, o_centered, o_sq, o_var = sem("rot_done"), sem("o_centered"), sem("o_sq"), sem("o_var")
        o_rms, o_normed = sem("o_rms"), sem("o_normed")
        f_ln, c_done, pooled, pool_step = sem("f_ln"), sem("c_done"), sem("pooled"), sem("pool_step")
        qzf_done, flog_done, fprob_done = sem("qzf_done"), sem("flog_done"), sem("fprob_done")
        w_high, w_low, h_low = sem("w_high"), sem("w_low"), sem("h_low")
        dve2, q_zero = sem("dve2"), sem("q_zero")
        groups20 = arena[:, S0 + 8480:S0 + 10400].rearrange("p (g v) -> p g v", v=RV)
        squares20 = region(17120, 20 * RV, "p (g v) -> p g v", v=RV)
        RET_OFF = (0, 512, 896, 1152, 1280)

        def norm_index(l, k):
            return 2 * l + k + 1

        block = ctx.enter_context(nc.Block())

        @block.sync
        def _(sp):
            sp.dma_start(xtok, a["x"][0].rearrange("(t p) d -> p t d", p=P)).then_inc(x_in, 16)
            for n, (src, _, _) in enumerate(units):
                if n >= NSLOT:
                    _, used, count = units[n - NSLOT]
                    sp.wait_ge(used, count)
                sp.dma_start(slot(n), src).then_inc(loaded[n % NSLOT], 16)
            for j in range(6):
                if j == 4:
                    sp.wait_ge(ym_done, MH)
                    sp.dma_start(arena[:, 8192:12288], x_d).then_inc(xre_in, 16)
                _, used, count = units[MOE_U + j - NSLOT]
                sp.wait_ge(used, count)
                sp.dma_start(expert_slot(j), expert_unit(sp, 0, j)).then_inc(loaded[(MOE_U + j) % NSLOT], 16)

            def load_expert(e, js):
                for j in js:
                    src = expert_unit(sp, e, j)
                    if j >= 6:
                        sp.wait_ge(gu_done, 4 * e + (j - 6) // 2 + 1)
                    elif j < 2:
                        sp.wait_ge(gu_done, 4 * (e - 1) + 4)
                    else:
                        sp.wait_ge(down_done, 2 * (e - 1) + j // 2)
                    sp.dma_start(expert_slot(j), src).then_inc(loaded[(MOE_U + j) % NSLOT], 16)

            with sp.Fori(0, NE - 1) as e:
                load_expert(e, range(6, 12))
                load_expert(e + 1, range(6))
            load_expert(NE - 1, range(6, 12))
            def layer_unit(l, n, first=False):
                for k, (name, col, cols) in enumerate(UNITS[n]):
                    rows, width = a[name].shape[1], a[name].shape[2]
                    offset = l * (rows * width) + col
                    if not isinstance(l, int):
                        sp.lower_val(offset * 4)
                    if k == 0 and n >= NSLOT2:
                        plan, stage, i = USED[n - NSLOT2]
                        sp.wait_ge(v_filled if plan is VL else a_filled, plan.layer(l).count(stage, i))
                    elif k == 0 and first:
                        if n == 0:
                            sp.wait_ge(gu_done, 4 * NE)
                        else:
                            sp.wait_ge(down_done, 2 * NE - (n == 1))
                    elif k == 0:
                        plan, stage, i = USED[n + LAYER_UNITS - NSLOT2]
                        sp.wait_ge(v_filled, plan.layer(l - 1).count(stage, i))
                    src = bass.AP(a[name].tensor, offset, [[width, P], [P * width, rows // P], [1, cols]])
                    sp.dma_start(slot2(n, rows // P, len(UNITS[n]), cols)[:, :, k, :], src).then_inc(loaded2[n % NSLOT2], 16)

            for n in range(NSLOT2):
                layer_unit(0, n, first=True)
            with sp.Fori(0, LAYERS - 1) as l:
                for n in range(NSLOT2, LAYER_UNITS):
                    layer_unit(l, n)
                for n in range(NSLOT2):
                    layer_unit(l + 1, n)
            for n in range(NSLOT2, LAYER_UNITS):
                layer_unit(LAYERS - 1, n)
            for t in range(TT):
                sp.wait_ge(v_freed, VF.count("out", 2 * t + 1))
                sp.dma_start(out[0, t * P:t * P + P, :], otile[:, t, :]).then_inc(out_sem, 16)
            sp.wait_ge(out_sem, 16 * TT)

        @block.gpsimd
        def _(pool):
            pool.memset(ident[:], 0.0).then_inc(pool_const, 1)
            pool.memset(flip[:], 0.0).then_inc(pool_const, 1)
            pool.memset(bmask[:], 1.0).then_inc(pool_const, 1)
            pool.wait_ge(pool_const, 3)
            pool.affine_select(out=ident[:], in_=ident[:], compare_op=ALU.not_equal, fill=1.0,
                               base=0, pattern=[[-1, P]], channel_multiplier=1).then_inc(pool_const, 1)
            pool.affine_select(out=flip[:], in_=flip[:], compare_op=ALU.not_equal, fill=1.0,
                               base=1 - P, pattern=[[1, P]], channel_multiplier=1).then_inc(pool_const, 1)
            pool.affine_select(out=bmask[:], in_=bmask[:], compare_op=ALU.is_ge, fill=0.0,
                               base=0, pattern=[[-4, 32]], channel_multiplier=1).then_inc(pool_const, 1)
            pool.wait_ge(pool_const, 6)
            pool.affine_select(out=bmask[:], in_=bmask[:], compare_op=ALU.is_ge, fill=0.0,
                               base=3, pattern=[[4, 32]], channel_multiplier=-1).then_inc(pool_const, 1)
            for i, nm in enumerate(("w_q_blk", "w_k_blk", "w_v_blk")):
                pool.dma_start(wraw[:, i, :, :], a[nm][0].rearrange("(h g) i j -> (g i) h j", h=MH)).then_inc(wraw_in, 16)
            pool.wait_ge(v_freed, V.count("bvec"))
            pool.dma_start(bvec_d, bvec).then_inc(bvec_out, 16)
            pool.wait_ge(bvec_out, 16)
            for h in range(AH):
                if h >= 1:
                    pool.wait_ge(v_filled, V.count(f"toep{h - 1}"))
                pool.dma_start(hankel[:, 0, 0:896], bass.AP(bvec_d.tensor, bvec_d.offset + h * DIFFS, [[1, P], [1, 896]])).then_inc(hankel_in, 16)
                pool.wait_ge(hankel_in, 16 * (h + 1))
            for u in range(MH * TT):
                jt = u % TT
                for d, way in ((0, 1), (1, -1)):
                    if jt < TT - 1:
                        pool.wait_ge(factor_done, 2 * ((TT - 1) * (u // TT) + jt) + d + 1)
                    else:
                        pool.wait_ge(a_freed, A.count(f"rows{u // TT}", d))
                    diagonal = E[:, u % 2, d, jt * P:jt * P + P]
                    pool.affine_select(out=diagonal, in_=diagonal, compare_op=ALU.is_ge, fill=0.0, base=0,
                                       pattern=[[way, P]], channel_multiplier=-way).then_inc(factor_cut, 1)
            pool.wait_ge(ym_done, MH)
            pool.iota(slots_iota, pattern=[[0, TT * 2], [1, CAP]], base=1, channel_multiplier=0,
                      allow_small_or_imprecise_dtypes=True).then_inc(iota_done, 1)
            pool.dma_start(metar[:], a["meta_2"].rearrange("t (c p) -> (t c) p", p=P)).then_inc(meta_in, 16)
            pool.dma_start(winv[:], a["const_winv"]).then_inc(meta_in, 16)
            pool.dma_start(wcorr[:], a["const_wcorr"]).then_inc(meta_in, 16)
            for l in range(LAYERS):
                pool.dma_start(bfc[:, l:l + 1], a["b_f_2"][l].rearrange("(h o) -> h o", o=1)).then_inc(meta_in, 16)
            pool.wait_ge(v_freed, V.count("rankE"))
            pool.wait_ge(a_freed, A.count("h2tok"))
            pool.dma_start(decay, a["const_decay"]).then_inc(const2_in, 16)
            pool.dma_start(cosT, a["const_cos"]).then_inc(const2_in, 16)
            pool.dma_start(sinT, a["const_sin"]).then_inc(const2_in, 16)
            pool.dma_start(rotm, a["const_rot"]).then_inc(const2_in, 16)
            pool.dma_start(tri, a["const_tri"]).then_inc(const2_in, 16)
            pool.memset(pwL, 0.0).then_inc(pw_zero, 1)
            pool.wait_ge(pw_zero, 1)
            W_ = PADW + L2
            steps = [0]

            def link(ins):
                steps[0] += 1
                ins.then_inc(pool_step, 1)
                pool.wait_ge(pool_step, steps[0])

            for l in range(LAYERS):

                for g in range(4):
                    r = 64 * (g % 2)
                    offset = l * (4 * 64 * 64) + g * 64 * 64
                    if g == 0:
                        pool.wait_ge(par_done, l + 1)
                    pool.dma_start(pwL[r:r + 64, g // 2, r:r + 64],
                                   bass.AP(a["pool_w_2"].tensor, offset, [[64, 64], [1, 64]])).then_inc(pw_in, 16)
                VLl, ALl = VL.layer(l), AL.layer(l)
                pool.wait_ge(a_filled, ALl.count("ro3"))
                link(pool.memset(upad[:, :, 0:PADW], 0.0))
                pool.wait_ge(a_freed, ALl.count("u"))

                def mean(rows, c, s, last=False):
                    link(pool.tensor_tensor(s[rows, PADW:2 * PADW], s[rows, PADW:2 * PADW], wcorr[rows, c, :], ALU.mult))
                    link(pool.tensor_scalar(s[rows, PADW:W_], s[rows, PADW:W_], winv[rows, c:c + 1], None, ALU.mult))
                    minus = pool.tensor_tensor(sumA[rows, c, PADW:W_], s[rows, PADW:W_], upad[rows, c, PADW:W_], ALU.subtract)
                    if last:
                        minus.then_inc(pooled, 1)
                    else:
                        link(minus)

                low, high, full = slice(0, 64), slice(64, 128), slice(0, 128)
                link(pool.tensor_tensor(sumA[:, :, 1:W_], upad[:, :, 1:W_], upad[:, :, 0:W_ - 1], ALU.add))
                link(pool.tensor_tensor(sumB[high, 3:W_], sumA[high, 0, 3:W_], sumA[high, 0, 1:W_ - 2], ALU.add))
                mean(low, 0, sumA[:, 0, :])
                mean(high, 0, sumB)
                link(pool.tensor_tensor(sumB[:, 3:W_], sumA[:, 1, 3:W_], sumA[:, 1, 1:W_ - 2], ALU.add))
                link(pool.tensor_tensor(sumA[:, 1, 7:W_], sumB[:, 7:W_], sumB[:, 3:W_ - 4], ALU.add))
                link(pool.tensor_tensor(sumB[high, 15:W_], sumA[high, 1, 15:W_], sumA[high, 1, 7:W_ - 8], ALU.add))
                mean(low, 1, sumA[:, 1, :])
                mean(high, 1, sumB, last=True)

        @block.scalar
        def _(act):
            def vec(rows, r, ap, n):
                act.dma_start(rows[r:r + n, :], ap.rearrange("(r p) -> r p", p=P)).then_inc(vecA_in if rows is rowsA and r < FIRST else vecB_in, 16)

            vec(rowsA, ROW_C, a["c"][0], 8)
            vec(rowsA, ROW_ADA, a["b_ada"][0], 48)
            vec(rowsA, ROW_N1, a["norm1_g"][0], 8)
            vec(rowsA, ROW_N2, a["norm2_g"][0], 8)
            for w in range(TAPS):
                vec(rowsA, ROW_CW + 4 * w, a["conv_w"][0, w], 4)
            vec(rowsA, ROW_CB, a["conv_b"][0], 4)
            vec(rowsA, ROW_MG, a["mlstm_norm_g"][0], 4)
            vec(rowsA, ROW_SK, a["mlstm_skip"][0], 4)
            for r, nm in ((ROW_QG, "q_norm_g"), (ROW_KG, "k_norm_g")):
                for half in range(2):
                    act.dma_start(rowsA[r:r + 1, AD * half:AD * half + AD], a[nm]).then_inc(vecB_in, 16)
            act.wait_ge(dve_const, 9)
            wg_src = w_in[:, :, 1024:1040].rearrange("p c (d k h) -> p c k d h", d=2, k=2)
            for k in range(2):
                for q in range(2):
                    for d in range(2):
                        act.dma_start(wgate[:, :, k, 32 * q + 4 * d:32 * q + 4 * d + 4], wg_src[:, :, k, d, :]).then_inc(gate_in, 16)
                    nm = ("b_igate", "b_fgate")[k]
                    act.dma_start(bgate[32 * q:32 * q + 8, k:k + 1], a[nm][0].rearrange("d (h o) -> (d h) o", o=1)).then_inc(gate_in, 16)
            act.dma_start(bval[0:32, :], a["rel_bias"]).then_inc(bias_in, 16)
            act.dma_start(bval[32:33, :], a["const_ones"][:, 0:AH]).then_inc(bias_in, 16)

            def take(stage, i=0):
                return A.take(act, abank, a_filled, stage, i)

            act.wait_ge(v_freed, V.count("colsA"))
            act.activation(cs[:], colsA[:, ROW_C:ROW_C + 8], ACT.Silu).then_inc(silu_c, 1)
            for c in range(KC):
                act.wait_ge(v_freed, V.count("xT", c))
                act.activation(sq[:, c, :], xT[:, c, :], ACT.Square).then_inc(sq_done, 1)
            vec(rowsB, 0, a["ln_emb_g_2"], 8)
            vec(rowsB, 8, a["ln_emb_b_2"], 8)
            for l in range(2):
                o = 16 + GROUP * l
                for nm, n in (("ret_gn_g_2", 3), ("pool_scale_2", 2), ("ln1_g_2", 8), ("ln1_b_2", 8), ("ln2_g_2", 8), ("ln2_b_2", 8)):
                    vec(rowsB, o, a[nm][l], n)
                    o += n
            act.dma_start(x_d, arena[:, R3:R3 + 4096]).then_inc(x_stored, 16)
            act.activation(rms1[:], take("ms1p")[:, :], ACT.Copy).then_inc(a_freed, 1)
            b = take("ms1")
            act.activation(rms1[:], b[:, :], ACT.Sqrt, bias=eps1[:, 0:1], scale=1.0 / D).then_inc(a_freed, 1)
            act.dma_start(btab, a["const_buckets"]).then_inc(bias_in, 16)
            for c in range(MH):
                b = take("sigo", c)
                act.activation(sigo[:, c, :], b[:, :], ACT.Sigmoid).then_inc(a_freed, 1)
            for t in range(TT):
                b = take("av", t)
                act.activation(av[:, t, :], b[:, :], ACT.Copy).then_inc(a_freed, 1)
            act.wait_ge(v_filled, V.count("gates"))
            for c in range(8):
                act.wait_ge(v_freed, V.count("qk", c))
                act.activation(asq[:, c, :], (aq if c < 4 else ak)[:, c % 4, :], ACT.Square).then_inc(asq_done, 1)
            act.wait_ge(v_freed, V.count("gates"))
            tmp = gates[0:40, 2, :]
            act.activation(tmp, gates[0:40, 1, :], ACT.Abs).then_inc(act_step, 1)
            act.wait_ge(act_step, 1)
            act.activation(tmp, tmp, ACT.Exp, scale=-1.0).then_inc(act_step, 1)
            act.wait_ge(act_step, 2)
            act.activation(tmp, tmp, ACT.Ln, bias=1.0).then_inc(logf_part, 1)
            for c in range(8):
                b = take("ss", c)
                act.activation(asq[:, c, :], b[:, :], ACT.Sqrt, bias=eps1[:, 0:1], scale=1.0 / AD).then_inc(a_freed, 1)
            act.wait_ge(m_done, 2)
            act.activation(gates[0:40, 4, :], gates[0:40, 4, :], ACT.Exp, scale=-1.0).then_inc(expm_done, 1)
            for u in range(AU + 1):
                if u < AU:
                    act.wait_ge(logits_done, u + 1)
                    if u >= 2:
                        act.wait_ge(a_filled, A.count("probT", u - 2))
                    act.activation(prob[:, u % 2, :], logit[:, u % 2, :], ACT.Exp, bias=ast[:, u % 4, 1:2],
                                   accum_out=ast[:, u % 4, 2:3]).then_inc(prob_done, 1)
                if u >= 1:
                    v = u - 1
                    b = take("probT", v)
                    if v >= 2:
                        act.wait_ge(v_filled, V.count(f"aout{v - 2}"))
                    act.activation(probT[:, v % 2, :], b[:, :], ACT.Copy).then_inc(a_freed, 1)
            for c in range(4):
                b = take("yaT", c)
                act.activation(yT[:, 4 + c, :], b[:, :], ACT.Copy).then_inc(a_freed, 1)
            for c in range(MH):
                act.wait_ge(conv_done, c + 1)
                act.activation(xc[:, c, :], xc[:, c, :], ACT.Silu).then_inc(xc_done, 1)
            for c in range(2 * MH):
                b = take("qkm", c)
                act.activation((qm if c < MH else km)[:, c % MH, :], b[:, :], ACT.Copy,
                               scale=1.0 if c < MH else 1.0 / math.sqrt(MD)).then_inc(a_freed, 1)
            act.wait_ge(gneg_done, 1)
            steps = 2
            for h in range(MH):
                for jt in range(TT):
                    u = h * TT + jt
                    for d in range(2):
                        b = take(f"rows{h}", d)
                        if u >= 2 and d == 0:
                            act.wait_ge(weight_done, u - 1)
                        elif u >= 2:
                            act.wait_ge(v_freed, V.count(f"score{(u - 2) // TT}", (u - 2) % TT))
                        lo, hi = (jt * P, S) if d == 0 else (0, jt * P + P)
                        r = 36 * d + h
                        diag = slice(jt * P, jt * P + P)
                        act.activation(E[:, u % 2, d, diag], b[:, diag], ACT.Relu, scale=-1.0,
                                       bias=gneg[:, jt, r:r + 1]).then_inc(act_step, 1)
                        rest = slice(jt * P + P, hi) if d == 0 else slice(0, jt * P)
                        if rest.start < rest.stop:
                            act.activation(E[:, u % 2, d, rest], b[:, rest], ACT.Exp, bias=gcol[:, jt, r:r + 1]).then_inc(act_step, 1)
                            steps += 1
                        steps += 1
                        act.wait_ge(act_step, steps)
                        act.activation(E[:, u % 2, d, diag], E[:, u % 2, d, diag], ACT.Exp, scale=-1.0)\
                           .then_inc(factor_done if jt < TT - 1 else a_freed, 1)
            for h in range(MH):
                for t in range(TT):
                    act.wait_ge(v_freed, V.count(f"hout{h}", 2 * t + 1))
                    n = TT * h + t
                    if n >= 4:
                        act.wait_ge(hsq_done, n - 3)
                    act.activation(rms1[:, n % 4 * P:n % 4 * P + P], htok[:, t, h * P:h * P + P], ACT.Square,
                                   accum_out=hst[:, 0, 4 * h + t:4 * h + t + 1]).then_inc(hsq_done, 1)
            act.wait_ge(hsq_done, MH * TT)
            act.activation(hst[:, 1, :], hst[:, 0, :], ACT.Sqrt, bias=eps1[:, 0:1], scale=1.0 / MD).then_inc(hrms_done, 1)
            act.dma_start(wrout[:], a["w_router"][0].rearrange("(c p) e -> p c e", p=P)).then_inc(rout_in, 16)
            act.dma_start(brout[:], a["b_router"]).then_inc(rout_in, 16)
            for c in range(KC):
                act.wait_ge(v_freed, V.count("mix", c))
                act.activation(sq2[:, c, :], x2[:, c, :], ACT.Square).then_inc(sq2_done, 1)
            act.activation(rms1[:], take("ms2p")[:, :], ACT.Copy).then_inc(a_freed, 1)
            b = take("ms2")
            act.activation(rms1[:], b[:, :], ACT.Sqrt, bias=eps1[:, 0:1], scale=1.0 / D).then_inc(a_freed, 1)
            for i in range(2 * TT):
                b = take("h2tok", i)
                act.activation(h2tok[:, i // 2, 512 * (i % 2):512 * (i % 2) + 512], b[:, :], ACT.Copy).then_inc(a_freed, 1)
            act.wait_ge(rexp_ready, 1)
            act.activation(rlog[:], rlog[:], ACT.Exp).then_inc(rexp_done, 1)

            def copy_tokens(n):
                act.wait_ge(gather_done, n)
                act.activation(arena[:, M0 + 4096:M0 + 4608], XIN_BANK[:, :], ACT.Copy).then_inc(xin_copied, 1)

            copy_tokens(1)
            with act.Fori(0, NE) as e:
                for g in range(2):
                    act.wait_ge(gu_done, 4 * e + 2 * g + 1)
                    act.activation(sg[:, g, :], G_BANK[g][:, :], ACT.Silu).then_inc(silu_done, 1)
                    if g == 0:
                        act.wait_ge(selT_done, e + 1)
                        act.activation(selT[:, 0, :], SELT_BANK[:, :], ACT.Copy).then_inc(selT_copied, 1)
                for g in range(2):
                    act.wait_ge(hT_done, 2 * e + g + 1)
                    act.activation(arena[:, M0 + 6656 + 512 * g:M0 + 7168 + 512 * g], HT_BANK[g][:, :], ACT.Copy).then_inc(hT_copied, 1)
                copy_tokens(e + 2)
                act.wait_ge(down_done, 2 * e + 2)
                for i in range(2):
                    act.activation(ysb[:, 0, 512 * i:512 * i + 512], Y_BANK[i][:, :], ACT.Copy).then_inc(y_copied, 1)
            def norm(plan, sum_stage, var_stage, src, squares, n, bias, high=None):
                part = plan.take(act, apair, a_filled, sum_stage + "p", 0)
                act.activation(halves(mu), part[:, :, 0:HW], ACT.Copy).then_inc(a_freed, 1)
                b = plan.take(act, apair, a_filled, sum_stage, 0)
                act.activation(halves(mu), b[:, :, 0:HW], ACT.Copy, scale=1.0 / D).then_inc(a_freed, 1)
                for c in range(KC):
                    act.wait_ge(centered, KC * n + c + 1)
                    act.activation(squares[:, c, :], src[:, c, :], ACT.Square).then_inc(sqx_done, 1)
                part = plan.take(act, apair, a_filled, var_stage + "p", 0)
                act.activation(halves(rstd), part[:, :, 0:HW], ACT.Copy).then_inc(a_freed, 1)
                b = plan.take(act, apair, a_filled, var_stage, 0)
                act.activation(halves(rstd), b[:, :, 0:HW], ACT.Sqrt, bias=eps2[:, 0:1], scale=1.0 / D).then_inc(a_freed, 1)
                for c in range(KC):
                    act.wait_ge(scaled, KC * n + c + 1)
                    dst = H[:, c, :] if high is None else high[:, c, :].bitcast(FR)
                    act.activation(dst, H[:, c, :], ACT.Identity, bias=bias[:, c:c + 1], scale=1.0).then_inc(normed, 1)

            norm(AE, "sum", "var", X0, x0sq, 0, colsB[:, 8:16])
            for l in range(LAYERS):
                VLl, ALl = VL.layer(l), AL.layer(l)

                def take(stage, i=0):
                    return ALl.take(act, apair, a_filled, stage, i)

                for j in range(4):
                    b = take("raw", j)
                    if j >= 2:
                        act.wait_ge(rot_done, 6 * l + 2 * j - 2)
                    act.activation(halves(raw[:, j % 2, :]), b[:, :, 0:HW], ACT.Copy).then_inc(a_freed, 1)
                for t in range(5):
                    n = P if t < TT else META
                    act.activation(vr[0:n, t, :], take("vr", t)[0:n, 0, 0:RH * RV], ACT.Copy).then_inc(a_freed, 1)
                for h in range(RH):
                    if h < 3:
                        act.activation(halves(sgr[:, h, :]), take(f"gr{h}")[:, :, 0:HW], ACT.Silu).then_inc(a_freed, 1)
                    b = flat(take(f"ro{h}"))
                    act.activation(otok[:, 0:TT, RV * h:RV * h + RV], b[:, 0:TT * RV].rearrange("p (t v) -> p t v", t=TT), ACT.Copy)
                    act.activation(otok[0:META, TT, RV * h:RV * h + RV], b[0:META, TT * RV:5 * RV], ACT.Copy).then_inc(a_freed, 1)
                for i in range(2):
                    b = take("u", i)
                    act.activation(upad[:, i, 2 * META:2 * META + HW], b[:, 0, 0:HW], ACT.Copy)
                    act.activation(upad[:, i, META:2 * META], b[:, 1, HW - META:HW], ACT.Copy)
                    act.activation(upad[:, i, 2 * META + HW:META + L2], b[:, 1, 0:HW - META], ACT.Copy).then_inc(a_freed, 1)
                act.wait_ge(v_freed, VLl.count("f"))
                for k, (src, fn, kw) in enumerate(((flin, ACT.Abs, {}), (fln, ACT.Exp, {"scale": -1.0}), (fln, ACT.Ln, {"bias": 1.0}))):
                    act.activation(fln, src, fn, **kw).then_inc(f_ln, 1)
                    if k < 2:
                        act.wait_ge(f_ln, 3 * l + k + 1)
                act.wait_ge(o_centered, l + 1)
                act.activation(squares20, groups20, ACT.Square).then_inc(o_sq, 1)
                for i in range(3):
                    act.activation(halves(kf[:, i, :]), take("kf", i)[:, :, 0:HW], ACT.Copy).then_inc(a_freed, 1)
                act.wait_ge(o_var, l + 1)
                act.activation(gst[:, 2, :], gst[:, 1, :], ACT.Sqrt, bias=eps2[:, 0:1], scale=1.0 / RV).then_inc(o_rms, 1)
                for t in range(TT):
                    act.activation(vf[:, t, :], take("vf", t)[:, 0, 0:FH * FD], ACT.Copy).then_inc(a_freed, 1)
                for i in range(2):
                    act.activation(mixT[:, 3 + i, :], flat(take("pm", i))[:, 0:L2], ACT.Copy, scale=colsL[:, PS + i:PS + i + 1]).then_inc(a_freed, 1)
                for u in range(FU + 2):
                    if u < FU:
                        h, i = divmod(u, 5)
                        if i == 0:
                            b = take(f"cb{h}")
                            if h >= 2:
                                act.wait_ge(v_freed, VLl.count(f"fs{u - 6}"))
                            act.activation(halves(cb[:, h % 2, :]), b[:, :, 0:HW], ACT.Copy).then_inc(a_freed, 1)
                        n, w = (P, META + P * (i + 1)) if i < TT else (META, META)
                        act.wait_ge(flog_done, FU * l + u + 1)
                        act.activation(flog[0:n, u % 3, 0:w], flog[0:n, u % 3, 0:w], ACT.Exp, bias=ast[0:n, u % 4, 1:2], scale=1.0,
                                       accum_out=ast[0:n, u % 4, 2:3]).then_inc(fprob_done, 1)
                    if u >= 2:
                        v = u - 2
                        i = v % 5
                        b = flat(take(f"fp{v}"))
                        if v >= 2:
                            act.wait_ge(v_filled, VLl.count(f"fo{v - 2}"))
                        if i < TT:
                            act.activation(fpT[:, v % 2, 0:P * (i + 1)], b[:, 0:P * (i + 1)], ACT.Copy)
                        n = P if i < TT else META
                        act.activation(fpT[0:META, v % 2, 512:512 + n], b[0:META, 512:512 + n], ACT.Copy).then_inc(a_freed, 1)
                for i in range(3):
                    act.activation(mixT[:, 5 + i, :], flat(take("ft", i))[:, 0:L2], ACT.Copy).then_inc(a_freed, 1)

                def weights_high(n):
                    m = FFN_U + n
                    act.wait_ge(loaded2[m % NSLOT2], 16 * (l * SLOT_LOADS[m % NSLOT2] + slot2_count(m)))
                    act.activation(weight_part(n, True).bitcast(FR), weight_part(n, False, ring2), ACT.Copy).then_inc(w_high, 1)

                weights_high(0)
                weights_high(1)
                norm(ALl, "sum0", "var0", X, xsq, norm_index(l, 0), colsL[:, LN1B:LN1B + KC], high=h_hi)
                for n in range(FC):
                    if n + 2 < FC:
                        weights_high(n + 2)
                    act.activation(halves(hidden[:, n, :]), take("fg", n)[:, :, 0:HW], ACT.Silu).then_inc(a_freed, 1)
                norm(ALl, "sum1", "var1", X, xsq, norm_index(l, 1), colsL[:, LN2B:LN2B + KC])

        @block.vector
        def _(dve):
            steps = [0]

            def link(ins):
                steps[0] += 1
                ins.then_inc(dve_step, 1)
                dve.wait_ge(dve_step, steps[0])

            def take(stage, i=0):
                return V.take(dve, vbank, v_filled, stage, i)

            dve.memset(ones[:], 1.0).then_inc(dve_const, 1)
            dve.memset(inv32[:], 1.0 / 32).then_inc(dve_const, 1)
            dve.memset(eps1[:], EPS1).then_inc(dve_const, 1)
            dve.memset(head_ones[:], 0.0).then_inc(dve_const, 1)
            dve.memset(wgate[:], 0.0).then_inc(dve_const, 1)
            dve.memset(bgate[:], 0.0).then_inc(dve_const, 1)
            dve.wait_ge(dve_const, 6)
            dve.memset(head_ones[0:64, 0:64], 1.0).then_inc(dve_const, 1)
            dve.memset(head_ones[64:128, 64:128], 1.0).then_inc(dve_const, 1)
            dve.memset(xm[:, :, 0:2], 0.0).then_inc(dve_const, 1)
            dve.memset(xm[:, :, S + 2:S + 4], 0.0).then_inc(dve_const, 1)
            for c in range(KC):
                dve.tensor_copy(xT[:, c, :], take("xT", c)[:, :]).then_inc(v_freed, 1)
            dve.tensor_copy(colsA[:, 0:FIRST], take("colsA")[:, 0:FIRST]).then_inc(v_freed, 1)
            dve.wait_ge(silu_c, 1)
            dve.tensor_copy(cs32[:], cs[:].rearrange("p (c o) -> p c o", o=1).broadcast_to([P, KC, 32])).then_inc(cs_ready, 1)

            def modulation(lo, hi):
                for i in range(lo, hi):
                    b = take(f"modrow{i}")
                    if i >= 2:
                        dve.wait_ge(v_filled, V.count(f"modcol{i - 2}"))
                    dve.tensor_copy(modr[:, i % 2, :], b[:, :]).then_inc(v_freed, 1)
                    f = slice(4 * i, 4 * i + 4)
                    dve.tensor_tensor(mod[:, f], take(f"modcol{i}")[:, 0:4], colsA[:, f], ALU.add).then_inc(v_freed, 1)

            modulation(0, 4)
            dve.wait_ge(v_freed, V.count("modcol3"))
            link(dve.scalar_tensor_tensor(g1s[:], mod[:, 8:16], 1.0, colsA[:, ROW_N1:ROW_N1 + 8], ALU.add, ALU.mult))
            dve.wait_ge(a_freed, A.count("ms1"))
            link(dve.reciprocal(rms1[:], rms1[:]))
            for c in range(KC):
                link(dve.tensor_tensor(hT[:, c, :], xT[:, c, :], rms1[:], ALU.mult))
                dve.tensor_scalar(hT[:, c, :], hT[:, c, :], g1s[:, c:c + 1], mod[:, c:c + 1], ALU.mult, ALU.add).then_inc(h_done, 1)
            for c in range(MH):
                dve.tensor_copy(xm[:, c, 2:S + 2], take("xm", c)[:, :]).then_inc(v_freed, 1)
            dve.wait_ge(x_stored, 16)
            for c in range(8):
                dve.tensor_copy((aq if c < 4 else ak)[:, c % 4, :], take("qk", c)[:, :]).then_inc(v_freed, 1)
            dve.wait_ge(gate_in, 16 * 6)
            for k in range(2):
                dve.tensor_scalar(gates[0:40, k, :], take("gates", k)[0:40, :], bgate[:, k:k + 1], None, ALU.add).then_inc(v_freed, 1)
            dve.tensor_copy(colsA[:, FIRST:ROWS_A], take("colsA2")[:, FIRST:ROWS_A]).then_inc(v_freed, 1)
            dve.tensor_copy(colsB[:], take("colsB")[:, 0:ROWS_B]).then_inc(v_freed, 1)
            modulation(4, 6)
            dve.wait_ge(logf_part, 1)
            link(dve.scalar_tensor_tensor(gates[0:40, 1, :], gates[0:40, 1, :], 0.0, gates[0:40, 2, :], ALU.min, ALU.subtract))
            dve.memset(gates[0:40, 3, :], 0.0)
            dve.memset(gates[0:40, 4, :], 0.0)
            dve.memset(negM[:], 0.0)
            link(dve.memset(gates[0:40, 2, :], 1.0))
            for q, way in ((0, 1), (32, -1)):
                rows = slice(q, q + 8)
                Bc = gates[rows, 4, ::way]
                link(dve.tensor_tensor_scan(Bc, gates[rows, 2, ::way], gates[rows, 1, ::way], 0.0, ALU.mult, ALU.add))
            for q, way in ((0, 1), (32, -1)):
                rows = slice(q, q + 8)
                link(dve.tensor_tensor(gates[rows, 3, :], gates[rows, 0, :], gates[rows, 4, :], ALU.subtract))
                link(dve.tensor_tensor_scan(negM[rows, ::way], gates[rows, 3, ::way], gates[rows, 3, ::way], 0.0, ALU.max, ALU.max))
                link(dve.tensor_tensor(gates[rows, 4, :], gates[rows, 4, :], negM[rows, :], ALU.add))
                dve.tensor_scalar(negM[rows, :], negM[rows, :], -1.0, None, ALU.mult).then_inc(m_done, 1)
            link(dve.tensor_scalar(qg8[:], colsA[:, ROW_QG:ROW_QG + 1], 1.0 / math.sqrt(AD), None, ALU.mult))
            for c in range(8):
                dve.wait_ge(a_freed, A.count("ss", c))
                link(dve.reciprocal(asq[:, c, :], asq[:, c, :]))
                x_ = (aq if c < 4 else ak)[:, c % 4, :]
                g_ = qg8[:, 0:1] if c < 4 else colsA[:, ROW_KG:ROW_KG + 1]
                link(dve.scalar_tensor_tensor(x_, x_, g_, asq[:, c, :], ALU.mult, ALU.mult))
                if c < 6:
                    modulation(6 + c, 7 + c)
            for i in range(3):
                lo, hi = 400 * i, min(400 * i + 400, DIFFS)
                dve.tensor_copy(bvec[:, lo:hi], take("bvec", i)[0:AH, 0:hi - lo]).then_inc(v_freed, 1)
            dve.tensor_copy(gcol[:], take("gcol")[:, 0:320].rearrange("p (k r) -> p k r", r=40)).then_inc(v_freed, 1)
            dve.wait_ge(v_freed, V.count("gcol"))
            dve.tensor_scalar(gneg[:], gcol[:, 0:TT, :], -1.0, None, ALU.mult).then_inc(gneg_done, 1)
            dve.memset(qz, 0.0).then_inc(qk_normed, 1)
            dve.wait_ge(qk_normed, 1)
            dve.wait_ge(bvec_out, 16)

            for u in range(AU + 2):
                if u < AU:
                    h, qt = divmod(u, TT)
                    if qt == 0:
                        if h >= 2:
                            dve.wait_ge(v_filled, V.count(f"logits{u - TT - 1}"))
                        rows = slice(AD * (h % 2), AD * (h % 2) + AD)
                        dve.tensor_copy(qz[rows, h % 2, :], aq[rows, h // 2, :]).then_inc(qz_done, 1)
                        for i in range(2):
                            dve.tensor_copy(toep[:, h % 2, 448 * i:448 * i + 448], take(f"toep{h}", i)[:, 0:448]).then_inc(v_freed, 1)
                        dve.wait_ge(v_freed, V.count(f"toep{h}"))
                    b = take(f"logits{u}")
                    if u >= 2:
                        dve.wait_ge(prob_done, u - 1)
                    off = 384 - P * qt
                    dve.tensor_tensor_reduce(out=logit[:, u % 2, :], in0=b[:, :], in1=toep[:, h % 2, off:off + S], scale=1.0,
                                             scalar=-3e38, op0=ALU.add, op1=ALU.max,
                                             accum_out=ast[:, u % 4, 0:1]).then_inc(v_freed, 1)
                    dve.wait_ge(v_freed, V.count(f"logits{u}"))
                    dve.tensor_scalar(ast[:, u % 4, 1:2], ast[:, u % 4, 0:1], -1.0, None, ALU.mult).then_inc(logits_done, 1)
                if u >= 2:
                    v = u - 2
                    h, qt = divmod(v, TT)
                    link(dve.reciprocal(ast[:, v % 4, 3:4], ast[:, v % 4, 2:3]))
                    b = take(f"aout{v}")
                    dve.tensor_scalar(atok[:, qt, AD * h:AD * h + AD], b[:, 0:AD], ast[:, v % 4, 3:4], None, ALU.mult).then_inc(v_freed, 1)
            dve.wait_ge(a_filled, A.count("yaT"))
            for c in range(MH):
                link(dve.tensor_scalar(xc[:, c, :], xm[:, c, 0:S], colsA[:, ROW_CW + c:ROW_CW + c + 1],
                                       colsA[:, ROW_CB + c:ROW_CB + c + 1], ALU.mult, ALU.add))
                for w in range(1, TAPS):
                    r = ROW_CW + 4 * w + c
                    tap = dve.scalar_tensor_tensor(xc[:, c, :], xm[:, c, w:w + S], colsA[:, r:r + 1], xc[:, c, :], ALU.mult, ALU.add)
                    if w < TAPS - 1:
                        link(tap)
                tap.then_inc(conv_done, 1)
            dve.wait_ge(wraw_in, 48)
            dve.wait_ge(pool_const, 7)
            for i in range(3):
                for h in range(MH):
                    dve.tensor_tensor(wbd[:, i, h, :].rearrange("p (g j) -> p g j", j=4),
                                      wraw[:, i, h:h + 1, :].broadcast_to([P, 32, 4]),
                                      bmask[:].rearrange("p (g o) -> p g o", o=1).broadcast_to([P, 32, 4]),
                                      ALU.mult).then_inc(wbd_done, 1)
            dve.memset(vm[:, :, :, MD:MD + 1], 1.0).then_inc(wbd_done, 1)
            for t in range(TT):
                dve.tensor_copy(vm[:, t, :, 0:MD], take("vm", t)[:, :].rearrange("p (h d) -> p h d", h=MH)).then_inc(v_freed, 1)
            for h in range(MH):
                for jt in range(TT):
                    u = h * TT + jt
                    b = take(f"score{h}", jt)
                    for d in range(2):
                        dve.wait_ge(factor_cut, 2 * u + d + 1)
                        lo, hi = (jt * P, S) if d == 0 else (0, jt * P + P)
                        dve.tensor_tensor(Wt(d, jt), b[:, lo:hi], E[:, u % 2, d, lo:hi], ALU.mult)\
                           .then_inc(weight_done if d == 0 else v_freed, 1)
                for t in range(TT):
                    hn = htok[:, t, h * P:h * P + P]
                    for d in range(2):
                        b = take(f"hout{h}", 2 * t + d)
                        e = 36 * d + h
                        link(dve.scalar_tensor_tensor(den[:, 0:1], b[:, MD:MD + 1], -1.0, gcol[:, TT + t, e:e + 1], ALU.mult, ALU.max))
                        link(dve.tensor_scalar(den[:, 0:1], b[:, MD:MD + 1], den[:, 0:1], None, ALU.max))
                        link(dve.reciprocal(den[:, 1:2], den[:, 0:1]))
                        if d == 0:
                            ins = dve.tensor_scalar(hn, b[:, 0:MD], den[:, 1:2], None, ALU.mult)
                        else:
                            ins = dve.scalar_tensor_tensor(hn, b[:, 0:MD], den[:, 1:2], hn, ALU.mult, ALU.add)
                        ins.then_inc(v_freed, 1)
                        dve.wait_ge(v_freed, V.count(f"hout{h}", 2 * t + d))
            dve.wait_ge(hrms_done, 1)
            link(dve.reciprocal(hst[:, 2, :], hst[:, 1, :]))
            for h in range(MH):
                for t in range(TT):
                    hn = htok[:, t, h * P:h * P + P]
                    dve.tensor_scalar(hn, hn, hst[:, 2, 4 * h + t:4 * h + t + 1], None, ALU.mult).then_inc(hnorm_done, 1)
            for h in range(MH):
                link(dve.tensor_scalar(xc[:, h, :], xc[:, h, :], colsA[:, ROW_SK + h:ROW_SK + h + 1], None, ALU.mult))
                b = take("ymT", h)
                dve.scalar_tensor_tensor(yT[:, h, :], b[:, :], colsA[:, ROW_MG + h:ROW_MG + h + 1], xc[:, h, :],
                                         ALU.mult, ALU.add).then_inc(v_freed, 1)
                dve.wait_ge(v_freed, V.count("ymT", h))
                dve.tensor_tensor(yT[:, h, :], yT[:, h, :], sigo[:, h, :], ALU.mult).then_inc(ym_done, 1)
            dve.wait_ge(xre_in, 16)
            for c in range(KC):
                dve.scalar_tensor_tensor(x2[:, c, :], take("mix", c)[:, :], mod[:, 16 + c:17 + c], xre[:, c, :],
                                         ALU.mult, ALU.add).then_inc(v_freed, 1)
            link(dve.scalar_tensor_tensor(g2s[:], mod[:, 32:40], 1.0, colsA[:, ROW_N2:ROW_N2 + 8], ALU.add, ALU.mult))
            dve.wait_ge(a_freed, A.count("ms2"))
            link(dve.reciprocal(rms1[:], rms1[:]))
            for c in range(KC):
                link(dve.tensor_tensor(h2T[:, c, :], x2[:, c, :], rms1[:], ALU.mult))
                dve.tensor_scalar(h2T[:, c, :], h2T[:, c, :], g2s[:, c:c + 1], mod[:, 24 + c:25 + c], ALU.mult, ALU.add).then_inc(h2_done, 1)
            dve.tensor_copy(rlog[:], take("route")[:, 0:TT * NE].rearrange("p (t e) -> p t e", e=NE)).then_inc(v_freed, 1)
            dve.wait_ge(v_freed, V.count("route"))
            link(dve.reduce_max(rst[:, 0, :], rlog[:], AX_X))

            def by_token(x, width):
                return x.rearrange("p (t o) -> p t o", o=1).broadcast_to([P, TT, width])

            dve.tensor_tensor(rlog[:], rlog[:], by_token(rst[:, 0, :], NE), ALU.subtract).then_inc(rexp_ready, 1)
            link(dve.memset(affT[:], 0.0))
            link(dve.memset(rankT[:], 0.0))
            dve.wait_ge(rexp_done, 1)
            link(dve.reduce_sum(rst[:, 1, :], rlog[:], AX_X))
            link(dve.reciprocal(rst[:, 2, :], rst[:, 1, :]))
            dve.tensor_tensor(affT[:, :, 0:NE], rlog[:], by_token(rst[:, 2, :], NE), ALU.mult).then_inc(aff_done, 1)
            dve.tensor_copy(aff, take("affE")[0:NE, :]).then_inc(v_freed, 1)
            dve.wait_ge(v_freed, V.count("affE"))
            for r in range(CAP // 8):
                left = aff if r == 0 else work
                link(dve.max(top8, left))
                link(dve.match_replace(out=work, in_to_replace=top8, in_values=left, imm_value=-1.0))
            link(dve.tensor_scalar(picked, work, 0.0, None, ALU.is_lt))
            link(dve.tensor_tensor_scan(work, picked, picked, 0.0, ALU.add, ALU.max))
            dve.tensor_tensor(work, work, picked, ALU.mult).then_inc(rank_done, 1)
            dve.tensor_copy(rankT[:, :, 0:NE], take("rankE")[:, 0:TT * NE].rearrange("p (t e) -> p t e", e=NE)).then_inc(v_freed, 1)
            dve.wait_ge(v_freed, V.count("rankE"))
            dve.wait_ge(a_freed, A.count("h2tok"))
            dve.memset(arena[:, R0:R0 + 4096], 0.0).then_inc(acc_done, 1)
            dve.wait_ge(iota_done, 1)

            def select(n, e):
                def flat(x):
                    return x.rearrange("p t a c -> p t (a c)")
                dve.tensor_tensor(flat(sel), flat(slots_iota), rankT[:, :, bass.ds(e, 1)].broadcast_to([P, TT, 2 * CAP]),
                                  ALU.is_equal).then_inc(sel_done, 1)
                dve.wait_ge(sel_done, 2 * n - 1)
                dve.tensor_tensor(flat(selg), flat(sel), affT[:, :, bass.ds(e, 1)].broadcast_to([P, TT, 2 * CAP]),
                                  ALU.mult).then_inc(sel_done, 1)

            select(1, 0)
            with dve.Fori(0, NE) as e:
                for g in range(2):
                    dve.wait_ge(gu_done, 4 * e + 2 * g + 2)
                    dve.wait_ge(silu_done, 2 * e + g + 1)
                    dve.tensor_tensor(hid[:, g, :], sg[:, g, :], U_BANK[g][:, :], ALU.mult).then_inc(hid_done, 1)
                    if g == 0:
                        dve.wait_ge(selT_done, e + 1)
                        select(e + 2, e + 1)
                for c in range(KC):
                    dve.wait_ge(scatter_done, 8 * e + c + 1)
                    dve.tensor_tensor(acc[:, c, :], acc[:, c, :], OUT_BANK[c % 4][:, :], ALU.add).then_inc(acc_done, 1)
            dve.wait_ge(acc_done, 8 * NE + 1)
            steps2 = [0]

            def link2(ins):
                steps2[0] += 1
                ins.then_inc(dve2, 1)
                dve.wait_ge(dve2, steps2[0])

            def norm(plan, sum_stage, var_stage, src, gain, after=None):
                dve.wait_ge(a_freed, plan.count(sum_stage))
                for c in range(KC):
                    dve.tensor_tensor(src[:, c, :], src[:, c, :], mu, ALU.subtract).then_inc(centered, 1)
                dve.wait_ge(a_freed, plan.count(var_stage))
                link2(dve.reciprocal(rstd, rstd))
                for c in range(KC):
                    dve.scalar_tensor_tensor(H[:, c, :], src[:, c, :], gain[:, c:c + 1], rstd, ALU.mult, ALU.mult).then_inc(scaled, 1)
                    if after is not None and c >= 2:
                        after(c - 2)

            dve.memset(eps2[:], EPS2).then_inc(x3_done, 1)
            for c in range(KC):
                dve.scalar_tensor_tensor(X0[:, c, 0:S], acc[:, c, :], mod[:, 40 + c:41 + c], x2[:, c, :],
                                         ALU.mult, ALU.add).then_inc(x3_done, 1)
            b = VE.take(dve, vpair, v_filled, "meta", 0)
            dve.tensor_copy(X0[:, :, S:L2], b[:, 0, 0:P].rearrange("p (t c) -> p c t", c=KC)).then_inc(v_freed, 1)
            norm(AE, "sum", "var", X0, colsB[:, 0:8])

            for l in range(LAYERS):
                VLl, ALl = VL.layer(l), AL.layer(l)

                def take(stage, i=0):
                    return VLl.take(dve, vpair, v_filled, stage, i)

                dve.wait_ge(normed, KC * norm_index(l, 0))
                dve.tensor_copy(colsL[:], colsB[:, 16 + GROUP * l:16 + GROUP * (l + 1)]).then_inc(par_done, 1)
                dve.memset(arena[:, S0 + 1584:S0 + 3696], 0.0).then_inc(q_zero, 1)
                dve.memset(otok[:, TT, :], 0.0).then_inc(q_zero, 1)
                dve.wait_ge(q_zero, 2 * l + 2)
                if l == 0:
                    dve.wait_ge(const2_in, 16 * 5)
                for j in range(4):
                    b = take("rot", j)
                    if j >= 1:
                        dve.wait_ge(rot_done, 6 * l + min(2 * j, j + 2))
                    dve.tensor_tensor(halves(rtmp[:, 0, :]), b[:, :, 0:HW], halves(sinT), ALU.mult).then_inc(v_freed, 1)
                    link2(dve.tensor_tensor(raw[:, j % 2, :], raw[:, j % 2, :], cosT, ALU.mult))
                    if j < 2:
                        for s in range(2):
                            rows = slice(64 * s, 64 * s + 64)
                            dve.tensor_tensor(qzr[rows, 2 * j + s, :], rtmp[rows, 0, :], raw[rows, j % 2, :], ALU.add).then_inc(rot_done, 1)
                    else:
                        dve.tensor_tensor(kr[:, j - 2, :], rtmp[:, 0, :], raw[:, j % 2, :], ALU.add).then_inc(rot_done, 1)
                for h in range(RH):
                    for t in range(5):
                        b = flat(take(f"rs{h}", t))
                        if h >= 1 and t == 0:
                            dve.wait_ge(a_filled, ALl.count(f"ro{h - 1}"))
                        o = RET_OFF[t]
                        if t < TT:
                            w = S - P * t
                            dve.tensor_tensor(retW[:, o:o + w], b[:, 0:w], decay[:, h, 0:w], ALU.mult).then_inc(v_freed, 1)
                        else:
                            dve.tensor_tensor(retW[0:META, o:o + S], b[0:META, 0:S], decay[0:META, h, META:L2], ALU.mult)
                            dve.tensor_tensor(retW[0:META, o + S:o + L2], b[0:META, S:L2], decay[0:META, h, 0:META], ALU.mult).then_inc(v_freed, 1)
                b = take("f")
                dve.wait_ge(a_filled, ALl.count(f"ro{RH - 1}"))
                dve.tensor_scalar(halves(flin), b[0:FH, :, 0:HW], bfc[:, l:l + 1], None, ALU.add).then_inc(v_freed, 1)
                def by_group(x):
                    return x.rearrange("p (g o) -> p g o", o=1).broadcast_to([P, 20, RV])

                dve.wait_ge(a_freed, ALl.count(f"ro{RH - 1}"))
                link2(dve.reduce_sum(gst[:, 0, :], groups20, AX_X))
                link2(dve.tensor_scalar(gst[:, 0, :], gst[:, 0, :], 1.0 / RV, None, ALU.mult))
                dve.tensor_tensor(groups20, groups20, by_group(gst[:, 0, :]), ALU.subtract).then_inc(o_centered, 1)
                for i in range(3):
                    dve.tensor_scalar(halves(qf[:, i, :]), take("qf", i)[:, :, 0:HW], 1.0 / math.sqrt(FD), None, ALU.mult).then_inc(v_freed, 1)
                dve.wait_ge(o_sq, l + 1)
                dve.reduce_sum(gst[:, 1, :], squares20, AX_X).then_inc(o_var, 1)
                dve.wait_ge(f_ln, 3 * (l + 1))
                link2(dve.scalar_tensor_tensor(flin, flin, 0.0, fln, ALU.min, ALU.subtract))
                link2(dve.tensor_tensor_scan(negc[:, 0:META], flin[:, S:L2], flin[:, S:L2], 0.0, ALU.add, ALU.min))
                link2(dve.tensor_tensor_scan(negc[:, META:L2], flin[:, 0:S], flin[:, 0:S], negc[:, META - 1:META], ALU.add, ALU.min))
                dve.tensor_scalar(negc, negc, -1.0, None, ALU.mult).then_inc(c_done, 1)
                dve.tensor_copy(vf[0:META, TT, :], take("vfm")[0:META, 0, 0:FH * FD]).then_inc(v_freed, 1)
                dve.wait_ge(o_rms, l + 1)
                link2(dve.reciprocal(gst[:, 3, :], gst[:, 2, :]))
                dve.tensor_tensor(groups20, groups20, by_group(gst[:, 3, :]), ALU.mult).then_inc(o_normed, 1)
                for i in range(3):
                    dve.scalar_tensor_tensor(mixT[:, i, :], flat(take("rt", i))[:, 0:L2], colsL[:, GN + i:GN + i + 1], sgr[:, i, :],
                                             ALU.mult, ALU.mult).then_inc(v_freed, 1)
                dve.wait_ge(a_filled, ALl.count("pm"))
                link2(dve.memset(arena[:, S0 + 5088:S0 + 6144], 0.0))
                for u in range(FU + 3):
                    if u < FU:
                        h, i = divmod(u, 5)
                        if i == 0:
                            if h >= 2:
                                dve.wait_ge(v_filled, VLl.count(f"fs{u - 6}"))
                            rows = slice(64 * (h % 2), 64 * (h % 2) + 64)
                            dve.tensor_copy(qzf[rows, h % 2, :], qf[rows, h // 2, :]).then_inc(qzf_done, 1)
                            dve.wait_ge(a_freed, ALl.count(f"cb{h}"))
                        n, w = (P, META + P * (i + 1)) if i < TT else (META, META)
                        b = flat(take(f"fs{u}"))
                        if u >= 3:
                            dve.wait_ge(a_filled, ALl.count(f"fp{u - 3}"))
                        dve.tensor_tensor_reduce(out=flog[0:n, u % 3, 0:w], in0=b[0:n, 0:w], in1=cb[0:n, h % 2, 0:w], scale=1.0,
                                                 scalar=-3e38, op0=ALU.add, op1=ALU.max,
                                                 accum_out=ast[0:n, u % 4, 0:1]).then_inc(v_freed, 1)
                        dve.wait_ge(v_freed, VLl.count(f"fs{u}"))
                        dve.tensor_scalar(ast[0:n, u % 4, 1:2], ast[0:n, u % 4, 0:1], -1.0, None, ALU.mult).then_inc(flog_done, 1)
                    if u >= 3:
                        v = u - 3
                        h, i = divmod(v, 5)
                        n = P if i < TT else META
                        link2(dve.reciprocal(ast[0:n, v % 4, 3:4], ast[0:n, v % 4, 2:3]))
                        b = take(f"fo{v}")
                        dve.tensor_scalar(ftok[0:n, i, FD * h:FD * h + FD], b[0:n, 0, 0:FD], ast[0:n, v % 4, 3:4], None, ALU.mult).then_inc(v_freed, 1)
                for m in range(KC):
                    dve.scalar_tensor_tensor(halves(X[:, m, :]), halves(H[:, m, :]), ALPHA, take("op", m)[:, :, 0:HW],
                                             ALU.mult, ALU.add).then_inc(v_freed, 1)

                def weights_low(n):
                    dve.wait_ge(w_high, FC * l + n + 1)
                    dve.tensor_tensor(weight_part(n, False).bitcast(FR), weight_part(n, False, ring2), weight_part(n, True), ALU.subtract).then_inc(w_low, 1)

                weights_low(0)
                weights_low(1)

                def stream_low(c):
                    dve.wait_ge(normed, KC * norm_index(l, 0) + c + 1)
                    dve.scalar_tensor_tensor(h_lo[:, c, :].bitcast(FR), H[:, c, :], colsL[:, LN1B + c:LN1B + c + 1], h_hi[:, c, :],
                                             ALU.add, ALU.subtract).then_inc(h_low, 1)

                norm(ALl, "sum0", "var0", X, colsL[:, LN1G:LN1G + KC], after=stream_low)
                stream_low(KC - 2)
                stream_low(KC - 1)
                for n in range(FC):
                    if n + 2 < FC:
                        weights_low(n + 2)
                    b = take("fu", n)
                    dve.wait_ge(a_freed, ALl.count("fg", n))
                    dve.tensor_tensor(halves(hidden[:, n, :]), halves(hidden[:, n, :]), b[:, :, 0:HW], ALU.mult).then_inc(v_freed, 1)
                for m in range(KC):
                    link2(dve.tensor_tensor(X[:, m, :], h_lo[:, m, :], h_hi[:, m, :], ALU.add))
                    dve.scalar_tensor_tensor(halves(X[:, m, :]), halves(X[:, m, :]), ALPHA, take("dn", m)[:, :, 0:HW],
                                             ALU.mult, ALU.add).then_inc(v_freed, 1)
                norm(ALl, "sum1", "var1", X, colsL[:, LN2G:LN2G + KC])
            for t in range(TT):
                for i in range(2):
                    b = VF.take(dve, vpair, v_filled, "out", 2 * t + i)
                    dve.tensor_copy(otile[:, t, 512 * i:512 * i + 512], b[:, 0, :]).then_inc(v_freed, 1)

        @block.tensor
        def _(pe):
            def vclaim(stage, i=0):
                return V.claim(pe, vbank, v_freed, stage, i)

            def aclaim(stage, i=0):
                return A.claim(pe, abank, a_freed, stage, i)

            def weights(n):
                pe.wait_ge(loaded[n % NSLOT], 16 * (n // NSLOT + 1))
                return slot(n)

            pe.wait_ge(pool_const, 5)
            pe.wait_ge(x_in, 16)
            for c in range(KC):
                b = vclaim("xT", c)
                for t in range(TT):
                    last = pe.transpose(b[:, t * P:t * P + P], xtok[:, t, c * P:c * P + P], ident[:])
                last.then_inc(v_filled, 1)

            pe.wait_ge(vecA_in, 16 * 3)
            pe.transpose(vclaim("colsA")[:, 0:FIRST], rowsA[0:FIRST, :], ident[0:FIRST, 0:FIRST]).then_inc(v_filled, 1)

            def modulation(lo, hi, unit):
                for i in range(lo, hi):
                    w = weights(unit + i - lo)
                    b = vclaim(f"modrow{i}")
                    for c in range(KC):
                        q = 32 * (c % 4)
                        last = pe.matmul(b[q:q + 32, :], cs32[:, c, :], w[:, c, :], start=c < 4, stop=c >= 4)
                    last.then_inc(v_filled, 1)
                    b = vclaim(f"modcol{i}")
                    pe.wait_ge(v_freed, V.count(f"modrow{i}"))
                    for j in range(4):
                        last = pe.matmul(b[:, j:j + 1], modr[:, i % 2, j * P:j * P + P], inv32[:], start=True, stop=True)
                    last.then_inc(v_filled, 1)

            pe.wait_ge(cs_ready, 1)
            pe.wait_ge(dve_const, 10)
            modulation(0, 4, ADA)
            b = aclaim("ms1p")
            for c in range(KC):
                pe.wait_ge(sq_done, c + 1)
                q = 32 * (c % 4)
                last = pe.matmul(b[q:q + 32, :], ones[:, 0:32], sq[:, c, :], start=c < 4, stop=c >= 4)
            last.then_inc(a_filled, 1)
            b = aclaim("ms1")
            pe.wait_ge(a_freed, A.count("ms1p"))
            pe.matmul(b[:, :], inv32[:].broadcast_to([P, P]), rms1[:], start=True, stop=True).then_inc(a_filled, 1)

            def by_features(b, w, col, done):
                for c in range(KC):
                    last = pe.matmul(b[:, :], w[:, c, col:col + P], hT[:, c, :], start=c == 0, stop=c == KC - 1)
                last.then_inc(done, 1)

            pe.wait_ge(h_done, KC)
            w = weights(XM_U)
            for m in range(MH):
                by_features(vclaim("xm", m), w, P * m, v_filled)
            w = weights(O_U)
            for m in range(MH):
                by_features(aclaim("sigo", m), w, P * m, a_filled)
            for m in range(8):
                w = weights(Q_U if m < 4 else K_U)
                by_features(vclaim("qk", m), w, P * (m % 4), v_filled)
            w = weights(V_U)
            pe.wait_ge(x_stored, 16)
            for t in range(TT):
                b = aclaim("av", t)
                for c in range(KC):
                    last = pe.matmul(b[:, :], hT[:, c, t * P:t * P + P], w[:, c, :], start=c == 0, stop=c == KC - 1)
                last.then_inc(a_filled, 1)
            pe.wait_ge(gate_in, 16 * 12)
            for k in range(2):
                b = vclaim("gates", k)
                for c in range(KC):
                    last = pe.matmul(b[0:40, :], wgate[:, c, k, :], hT[:, c, :], start=c == 0, stop=c == KC - 1)
                last.then_inc(v_filled, 1)
            pe.wait_ge(vecB_in, 16 * (1 + TAPS + 3 + 4 + 2 + 12))
            pe.transpose(vclaim("colsA2")[:, FIRST:ROWS_A], rowsA[FIRST:ROWS_A, :], ident[FIRST:ROWS_A, FIRST:ROWS_A]).then_inc(v_filled, 1)
            pe.transpose(vclaim("colsB")[:, 0:ROWS_B], rowsB[:], ident[0:ROWS_B, 0:ROWS_B]).then_inc(v_filled, 1)
            modulation(4, 6, ADA2)
            for m in range(8):
                pe.wait_ge(asq_done, m + 1)
                pe.matmul(aclaim("ss", m)[:, :], head_ones[:], asq[:, m, :], start=True, stop=True).then_inc(a_filled, 1)
            modulation(6, 12, ADA2 + 2)
            pe.wait_ge(bias_in, 48)
            for i in range(3):
                lo, hi = 400 * i, min(400 * i + 400, DIFFS)
                pe.matmul(vclaim("bvec", i)[0:AH, 0:hi - lo], bval[:], btab[:, lo:hi], start=True, stop=True).then_inc(v_filled, 1)
            b = vclaim("gcol")
            pe.wait_ge(m_done, 2)
            pe.wait_ge(expm_done, 1)
            for k in range(2 * TT):
                src = gates[0:40, 3 + k // TT, (k % TT) * P:(k % TT) * P + P]
                last = pe.transpose(b[:, 40 * k:40 * k + 40], src, ident[0:40, 0:40])
            last.then_inc(v_filled, 1)
            pe.wait_ge(qk_normed, 1)
            for u in range(AU + 2):
                if u < AU:
                    h, qt = divmod(u, TT)
                    if qt == 0:
                        pe.wait_ge(hankel_in, 16 * (h + 1))
                        for i in range(2):
                            pe.matmul(vclaim(f"toep{h}", i)[:, 0:448], flip[:], hankel[:, 0, 448 * i:448 * i + 448],
                                      start=True, stop=True).then_inc(v_filled, 1)
                        pe.wait_ge(qz_done, h + 1)
                    b = vclaim(f"logits{u}")
                    pe.matmul(b[:, :], qz[:, h % 2, qt * P:qt * P + P], ak[:, h // 2, :], start=True, stop=True).then_inc(v_filled, 1)
                if 1 <= u <= AU:
                    v = u - 1
                    b = aclaim("probT", v)
                    pe.wait_ge(prob_done, v + 1)
                    for kt in range(TT):
                        last = pe.transpose(b[:, kt * P:kt * P + P], prob[:, v % 2, kt * P:kt * P + P], ident[:])
                    last.then_inc(a_filled, 1)
                if u >= 2:
                    v = u - 2
                    h = v // TT
                    b = vclaim(f"aout{v}")
                    pe.wait_ge(a_freed, A.count("probT", v))
                    for kt in range(TT):
                        last = pe.matmul(b[:, 0:AD], probT[:, v % 2, kt * P:kt * P + P], av[:, kt, AD * h:AD * h + AD],
                                         start=kt == 0, stop=kt == TT - 1)
                    last.then_inc(v_filled, 1)
            pe.wait_ge(v_freed, V.count(f"aout{AU - 1}"))
            for c in range(4):
                b = aclaim("yaT", c)
                for t in range(TT):
                    last = pe.transpose(b[:, t * P:t * P + P], atok[:, t, c * P:c * P + P], ident[:])
                last.then_inc(a_filled, 1)
            pe.wait_ge(wbd_done, 3 * MH + 1)
            for m in range(2 * MH):
                pe.wait_ge(xc_done, m % MH + 1)
                pe.matmul(aclaim("qkm", m)[:, :], wbd[:, m // MH, m % MH, :], xc[:, m % MH, :], start=True, stop=True).then_inc(a_filled, 1)
            for t in range(TT):
                b = vclaim("vm", t)
                for h in range(MH):
                    last = pe.matmul(b[:, h * P:h * P + P], xm[:, h, 2 + t * P:2 + t * P + P], wbd[:, 2, h, :], start=True, stop=True)
                last.then_inc(v_filled, 1)
            for h in range(MH):
                for d in range(2):
                    b = aclaim(f"rows{h}", d)
                    r = 36 * d + h
                    pe.matmul(b[:, :], ident[0:40, r:r + 1].broadcast_to([40, P]), negM[:], start=True, stop=True).then_inc(a_filled, 1)
                for jt in range(TT):
                    b = vclaim(f"score{h}", jt)
                    if jt == 0:
                        pe.wait_ge(a_freed, A.count("qkm"))
                    pe.matmul(b[:, :], km[:, h, jt * P:jt * P + P], qm[:, h, :], start=True, stop=True).then_inc(v_filled, 1)
                for t in range(TT):
                    for d in range(2):
                        b = vclaim(f"hout{h}", 2 * t + d)
                        tiles = range(t + 1) if d == 0 else range(t, TT)
                        if d == 0:
                            pe.wait_ge(weight_done, TT * h + max(tiles) + 1)
                        else:
                            pe.wait_ge(v_freed, V.count(f"score{h}", max(tiles)))
                        for jt in tiles:
                            at = (t - jt if d == 0 else t) * P
                            last = pe.matmul(b[:, 0:MD + 1], Wt(d, jt)[:, at:at + P], vm[:, jt, h, :],
                                             start=jt == tiles[0], stop=jt == tiles[-1])
                        last.then_inc(v_filled, 1)
            for h in range(MH):
                b = vclaim("ymT", h)
                for t in range(TT):
                    pe.wait_ge(hnorm_done, TT * h + t + 1)
                    last = pe.transpose(b[:, t * P:t * P + P], htok[:, t, h * P:h * P + P], ident[:])
                last.then_inc(v_filled, 1)
            pe.wait_ge(ym_done, MH)
            pe.wait_ge(a_freed, A.count("yaT"))
            for m in range(KC):
                w = weights(OUT_U + m // 4)
                b = vclaim("mix", m)
                for c in range(KC):
                    last = pe.matmul(b[:, :], w[:, c, P * (m % 4):P * (m % 4) + P], yT[:, c, :], start=c == 0, stop=c == KC - 1)
                last.then_inc(v_filled, 1)
            b = aclaim("ms2p")
            for c in range(KC):
                pe.wait_ge(sq2_done, c + 1)
                q = 32 * (c % 4)
                last = pe.matmul(b[q:q + 32, :], ones[:, 0:32], sq2[:, c, :], start=c < 4, stop=c >= 4)
            last.then_inc(a_filled, 1)
            b = aclaim("ms2")
            pe.wait_ge(a_freed, A.count("ms2p"))
            pe.matmul(b[:, :], inv32[:].broadcast_to([P, P]), rms1[:], start=True, stop=True).then_inc(a_filled, 1)
            pe.wait_ge(h2_done, KC)
            for i in range(2 * TT):
                b = aclaim("h2tok", i)
                for j in range(4):
                    c = 4 * (i % 2) + j
                    last = pe.transpose(b[:, j * P:j * P + P], h2T[:, c, (i // 2) * P:(i // 2) * P + P], ident[:])
                last.then_inc(a_filled, 1)
            pe.wait_ge(rout_in, 32)
            b = vclaim("route")
            for t in range(TT):
                for c in range(KC):
                    pe.matmul(b[:, NE * t:NE * t + NE], h2T[:, c, t * P:t * P + P], wrout[:, c, :], start=c == 0, stop=False)
                last = pe.matmul(b[:, NE * t:NE * t + NE], ones[0:1, :], brout[:], start=False, stop=True)
            last.then_inc(v_filled, 1)
            b = vclaim("affE")
            pe.wait_ge(aff_done, 1)
            for t in range(TT):
                last = pe.transpose(b[0:NE, t * P:t * P + P], affT[:, t, 0:NE], ident[:])
            last.then_inc(v_filled, 1)
            b = vclaim("rankE")
            pe.wait_ge(rank_done, 1)
            for t in range(TT):
                last = pe.transpose(b[:, NE * t:NE * t + NE], work[:, t * P:t * P + P], ident[0:NE, 0:NE])
            last.then_inc(v_filled, 1)

            pe.wait_ge(v_freed, V.count("rankE"))
            pe.wait_ge(a_freed, A.count("h2tok"))

            def gather(n):
                pe.wait_ge(sel_done, 2 * n - 1)
                for c in range(KC):
                    for t in range(TT):
                        last = pe.matmul(XIN_BANK[:, CAP * c:CAP * c + CAP], h2tok[:, t, c * P:c * P + P], sel[:, t, 0, :],
                                         start=t == 0, stop=t == TT - 1)
                last.then_inc(gather_done, 1)

            def expert_weights(e, j):
                pe.wait_ge(loaded[(MOE_U + j) % NSLOT], expert_loaded(e, j))
                return expert_slot(j)

            def up(e, j, bank):
                for r in range(2):
                    w = expert_weights(e, j + r)
                    for c in range(4):
                        for blk in range(2):
                            last = pe.matmul(bank[CAP * blk:CAP * blk + CAP, :], xin[:, 4 * r + c, :],
                                             w[:, c, 512 * blk:512 * blk + 512], start=r + c == 0, stop=r + c == 4)
                last.then_inc(gu_done, 1)

            def transpose_hidden(e, g):
                pe.wait_ge(hid_done, 2 * e + g + 1)
                for j in range(4):
                    last = pe.transpose(HT_BANK[g][:, j * P:j * P + P], hid[:, g, j * P:j * P + P], ident[:])
                last.then_inc(hT_done, 1)

            def down(e, g):
                pe.wait_ge(hT_copied, 2 * e + g + 1)
                w = [expert_weights(e, 8 + 2 * g + blk) for blk in range(2)]
                for j in range(4):
                    for half in range(2):
                        for blk in range(2):
                            last = pe.matmul(Y_BANK[half][CAP * blk:CAP * blk + CAP, :], hidT[:, g, j, CAP * blk:CAP * blk + CAP],
                                             w[blk][:, j, 512 * half:512 * half + 512], start=g + j == 0, stop=g == 1 and j == 3)
                last.then_inc(down_done, 1)

            gather(1)
            with pe.Fori(0, NE) as e:
                pe.wait_ge(xin_copied, e + 1)
                up(e, 0, G_BANK[0])
                pe.wait_ge(sel_done, 2 * e + 2)
                for t in range(TT):
                    last = pe.transpose(SELT_BANK[:, t * P:t * P + P], selg[:, t, :, :].rearrange("p a c -> p (a c)"), ident[:])
                last.then_inc(selT_done, 1)
                up(e, 2, U_BANK[0])
                pe.wait_ge(acc_done, 8 * e + 1)
                up(e, 4, G_BANK[1])
                up(e, 6, U_BANK[1])
                transpose_hidden(e, 0)
                down(e, 0)
                transpose_hidden(e, 1)
                gather(e + 2)
                down(e, 1)
                pe.wait_ge(y_copied, 2 * e + 2)
                pe.wait_ge(selT_copied, e + 1)
                for c in range(KC):
                    if c >= 4:
                        pe.wait_ge(acc_done, 8 * e + c - 2)
                    pe.matmul(OUT_BANK[c % 4][:, :], ysb[:, 0, c * P:c * P + P], selT[:, 0, :], start=True, stop=True).then_inc(scatter_done, 1)
            pe.wait_ge(acc_done, 8 * NE + 1)
            pe.wait_ge(xin_copied, NE + 1)
            pe.wait_ge(meta_in, 16 * (3 + LAYERS))
            b = VE.claim(pe, vpair, v_freed, "meta", 0)
            pe.transpose(b[:, 0, 0:P], metar[:], ident[:]).then_inc(v_filled, 1)

            def column_sums(plan, stage, src, part, ready=None):
                b = plan.claim(pe, apair, a_freed, stage + "p", 0)
                for c in range(KC):
                    if ready is not None:
                        ready(c)
                    q = 32 * (c % 4)
                    for k in range(2):
                        last = pe.matmul(b[q:q + 32, k, 0:HW], ones[:, 0:32], halves(src[:, c, :])[:, k, :], start=c < 4, stop=c >= 4)
                last.then_inc(a_filled, 1)
                b = plan.claim(pe, apair, a_freed, stage, 0)
                pe.wait_ge(a_freed, plan.count(stage + "p"))
                for k in range(2):
                    last = pe.matmul(b[:, k, 0:HW], inv32[:].broadcast_to([P, P]), halves(part)[:, k, :], start=True, stop=True)
                last.then_inc(a_filled, 1)

            def squares_ready(n):
                return lambda c: pe.wait_ge(sqx_done, KC * n + c + 1)

            pe.wait_ge(v_freed, VE.count("meta"))
            column_sums(AE, "sum", X0, mu)
            column_sums(AE, "var", x0sq, rstd, squares_ready(0))

            for l in range(LAYERS):
                VLl, ALl = VL.layer(l), AL.layer(l)

                def vclaim(stage, i=0):
                    return VLl.claim(pe, vpair, v_freed, stage, i)

                def aclaim(stage, i=0):
                    return ALl.claim(pe, apair, a_freed, stage, i)

                def weights(n):
                    pe.wait_ge(loaded2[n % NSLOT2], 16 * (l * SLOT_LOADS[n % NSLOT2] + slot2_count(n)))
                    cols = UNITS[n][0][2]
                    return slot2(n, a[UNITS[n][0][0]].shape[1] // P, len(UNITS[n]), cols)

                def project(b, w, part, col, src, m=P):
                    chunks = w.shape[1]
                    for c in range(chunks):
                        for k in range(2):
                            last = pe.matmul(b[0:m, k, 0:HW], w[:, c, part, col:col + m], halves(src[:, c, :])[:, k, :],
                                             start=c == 0, stop=c == chunks - 1)
                    return last

                def project_tokens(b, w, col, n, t):
                    m = P if t < TT else META
                    for c in range(KC):
                        last = pe.matmul(b[0:m, 0, 0:n], H[:, c, P * t:P * t + m], w[:, c, 0, col:col + n], start=c == 0, stop=c == KC - 1)
                    return last

                def turn(b, src, i):
                    for t in range(TT):
                        pe.transpose(b[:, P * t:P * t + P], src[:, t, P * i:P * i + P], ident[:])
                    return pe.transpose(b[:, S:L2], src[0:META, TT, P * i:P * i + P], ident[0:META, 0:META])

                w = weights(0)

                def raw_pair(j):
                    b = aclaim("raw", j)
                    for c in range(KC):
                        if j == 0:
                            pe.wait_ge(normed, KC * (norm_index(l, 0) - 1) + c + 1)
                        for s in range(2):
                            col = RH * RK * (j // 2) + 2 * RK * (j % 2) + RK * s
                            for k in range(2):
                                last = pe.matmul(b[64 * s:64 * s + 64, k, 0:HW], w[:, c, 0, col:col + 64], halves(H[:, c, :])[:, k, :],
                                                 start=c == 0, stop=c == KC - 1)
                    last.then_inc(a_filled, 1)

                def rotate_pair(j):
                    if l == 0 and j == 0:
                        pe.wait_ge(const2_in, 16 * 5)
                    b = vclaim("rot", j)
                    pe.wait_ge(a_freed, ALl.count("raw", j))
                    for k in range(2):
                        last = pe.matmul(b[:, k, 0:HW], rotm, halves(raw[:, j % 2, :])[:, k, :], start=True, stop=True)
                    last.then_inc(v_filled, 1)

                raw_pair(0)
                raw_pair(1)
                rotate_pair(0)
                raw_pair(2)
                rotate_pair(1)
                raw_pair(3)
                rotate_pair(2)
                rotate_pair(3)
                for t in range(5):
                    project_tokens(aclaim("vr", t), w, 2 * RH * RK, RH * RV, t).then_inc(a_filled, 1)
                pe.wait_ge(rot_done, 6 * (l + 1))
                pe.wait_ge(a_freed, ALl.count("vr"))
                for h in range(RH):
                    for t in range(5):
                        b = flat(vclaim(f"rs{h}", t))
                        if t < TT:
                            last = pe.matmul(b[:, 0:S - P * t], kr[:, h // 2, P * t:P * t + P], qzr[:, h, P * t:S], start=True, stop=True)
                        else:
                            pe.matmul(b[0:META, 0:S], kr[:, h // 2, S:L2], qzr[:, h, 0:S], start=True, stop=True)
                            last = pe.matmul(b[0:META, S:L2], kr[:, h // 2, S:L2], qzr[:, h, S:L2], start=True, stop=True)
                        last.then_inc(v_filled, 1)
                    if h < 3:
                        project(aclaim(f"gr{h}"), weights(1), 0, P * h, H).then_inc(a_filled, 1)
                    else:
                        project(vclaim("f"), weights(2), 0, 0, H, m=FH).then_inc(v_filled, 1)
                    b = flat(aclaim(f"ro{h}"))
                    pe.wait_ge(v_freed, VLl.count(f"rs{h}"))
                    hv = slice(RV * h, RV * h + RV)
                    for i in range(TT):
                        for t in range(i + 1):
                            o = RET_OFF[t] + P * (i - t)
                            pe.matmul(b[:, RV * i:RV * i + RV], retW[:, o:o + P], vr[:, t, hv], start=t == 0, stop=False)
                        o = RET_OFF[TT] + P * i
                        pe.matmul(b[:, RV * i:RV * i + RV], retW[0:META, o:o + P], vr[0:META, TT, hv], start=False, stop=True)
                    o = RET_OFF[TT] + S
                    pe.matmul(b[0:META, RV * TT:RV * 5], retW[0:META, o:o + META], vr[0:META, TT, hv], start=True, stop=True).then_inc(a_filled, 1)
                w = weights(1)
                for i in range(2):
                    project(aclaim("u", i), w, 0, RH * RV + P * i, H).then_inc(a_filled, 1)
                w = weights(3)
                for i in range(3):
                    project(vclaim("qf", i), w, 0, P * i, H).then_inc(v_filled, 1)
                w = weights(4)
                for i in range(3):
                    project(aclaim("kf", i), w, 0, P * i, H).then_inc(a_filled, 1)
                w = weights(5)
                for t in range(TT):
                    project_tokens(aclaim("vf", t), w, 0, FH * FD, t).then_inc(a_filled, 1)
                project_tokens(vclaim("vfm"), w, 0, FH * FD, TT).then_inc(v_filled, 1)
                for i in range(3):
                    b = flat(vclaim("rt", i))
                    pe.wait_ge(o_normed, l + 1)
                    turn(b, otok, i).then_inc(v_filled, 1)
                for i in range(2):
                    b = flat(aclaim("pm", i))
                    pe.wait_ge(pooled, l + 1)
                    pe.wait_ge(pw_in, 64 * (l + 1))
                    pe.matmul(b[:, 0:S], pwL[:, i, :], sumA[:, i, 2 * META:META + L2], start=True, stop=True)
                    pe.matmul(b[:, S:L2], pwL[:, i, :], sumA[:, i, META:2 * META], start=True, stop=True).then_inc(a_filled, 1)
                for u in range(FU + 3):
                    if u < FU:
                        h, i = divmod(u, 5)
                        if i == 0:
                            b = aclaim(f"cb{h}")
                            pe.wait_ge(c_done, l + 1)
                            for k in range(2):
                                last = pe.matmul(b[:, k, 0:HW], ident[0:FH, h:h + 1].broadcast_to([FH, P]), halves(negc)[:, k, :], start=True, stop=True)
                            last.then_inc(a_filled, 1)
                            pe.wait_ge(qzf_done, FH * l + h + 1)
                            pe.wait_ge(a_freed, ALl.count("kf"))
                        b = flat(vclaim(f"fs{u}"))
                        keys = kf[:, h // 2, :]
                        if i < TT:
                            q = qzf[:, h % 2, P * i:P * i + P]
                            pe.matmul(b[:, 0:META], q, keys[:, S:L2], start=True, stop=True)
                            if i > 0:
                                pe.matmul(b[:, META:META + P * i], q, keys[:, 0:P * i], start=True, stop=True)
                            lo, cut = P * i, min(P, S - META - P * i)
                            for x0, x1 in ((0, cut), (cut, P)):
                                if x1 > x0:
                                    dst = b[:, META + lo + x0:META + lo + x1]
                                    pe.matmul(dst, q, keys[:, lo + x0:lo + x1], start=True, stop=False)
                                    last = pe.matmul(dst, ident[:], tri[:, x0:x1], start=False, stop=True)
                        else:
                            pe.matmul(b[0:META, 0:META], qzf[:, h % 2, S:L2], keys[:, S:L2], start=True, stop=False)
                            last = pe.matmul(b[0:META, 0:META], ident[0:META, 0:META], tri[0:META, 0:META], start=False, stop=True)
                        last.then_inc(v_filled, 1)
                    if 2 <= u < FU + 2:
                        v = u - 2
                        i = v % 5
                        b = flat(aclaim(f"fp{v}"))
                        pe.wait_ge(fprob_done, FU * l + v + 1)
                        n = P if i < TT else META
                        if i < TT:
                            for t in range(i + 1):
                                pe.transpose(b[:, P * t:P * t + P], flog[:, v % 3, META + P * t:META + P * t + P], ident[:])
                        pe.transpose(b[0:META, S:S + n], flog[0:n, v % 3, 0:META], ident[0:n, 0:n]).then_inc(a_filled, 1)
                    if u >= 3:
                        v = u - 3
                        h, i = divmod(v, 5)
                        b = flat(vclaim(f"fo{v}"))
                        if v == 0:
                            pe.wait_ge(v_freed, VLl.count("vfm"))
                        pe.wait_ge(a_freed, ALl.count(f"fp{v}"))
                        n = P if i < TT else META
                        hv = slice(FD * h, FD * h + FD)
                        if i < TT:
                            for t in range(i + 1):
                                pe.matmul(b[:, 0:FD], fpT[:, v % 2, P * t:P * t + P], vf[:, t, hv], start=t == 0, stop=False)
                        pe.matmul(b[0:n, 0:FD], fpT[0:META, v % 2, S:S + n], vf[0:META, TT, hv], start=i == TT, stop=True).then_inc(v_filled, 1)
                for i in range(3):
                    b = flat(aclaim("ft", i))
                    pe.wait_ge(v_freed, VLl.count(f"fo{FU - 1}"))
                    turn(b, ftok, i).then_inc(a_filled, 1)
                for m in range(KC):
                    w = weights(6 + m // 2)
                    b = vclaim("op", m)
                    if m == 0:
                        pe.wait_ge(a_freed, ALl.count("ft"))
                        pe.wait_ge(v_freed, VLl.count("rt"))
                    project(b, w, 0, P * (m % 2), mixT).then_inc(v_filled, 1)
                column_sums(ALl, "sum0", X, mu, lambda c: pe.wait_ge(v_freed, VLl.count("op", c)))
                column_sums(ALl, "var0", xsq, rstd, squares_ready(norm_index(l, 0)))
                def project_parts(b, n, part):
                    w_hi, w_lo = (weight_part(n, high).bitcast(FR).rearrange("p (c k n) -> p c k n", c=KC, k=2) for high in (True, False))
                    for c in range(KC):
                        if n + part == 0:
                            pe.wait_ge(h_low, KC * l + c + 1)
                        for i, (w, x) in enumerate(((w_hi, h_hi), (w_hi, h_lo), (w_lo, h_hi))):
                            for k in range(2):
                                last = pe.matmul(b[:, k, 0:HW], w[:, c, part, :], halves(x[:, c, :])[:, k, :].bitcast(FR),
                                                 start=c == 0 and i == 0, stop=c == KC - 1 and i == 2)
                    return last

                for n in range(FC):
                    pe.wait_ge(w_low, FC * l + n + 1)
                    project_parts(aclaim("fg", n), n, 0).then_inc(a_filled, 1)
                    project_parts(vclaim("fu", n), n, 1).then_inc(v_filled, 1)
                for m in range(KC):
                    w = weights(DOWN_U + m // 2)
                    b = vclaim("dn", m)
                    pe.wait_ge(v_freed, VLl.count("fu"))
                    project(b, w, 0, P * (m % 2), hidden).then_inc(v_filled, 1)
                column_sums(ALl, "sum1", X, mu, lambda c: pe.wait_ge(v_freed, VLl.count("dn", c)))
                column_sums(ALl, "var1", xsq, rstd, squares_ready(norm_index(l, 1)))
            pe.wait_ge(normed, KC * norm_index(LAYERS, 0))
            for i in range(2 * TT):
                b = VF.claim(pe, vpair, v_freed, "out", i)
                for j in range(4):
                    last = pe.transpose(b[:, 0, P * j:P * j + P], H[:, 4 * (i % 2) + j, P * (i // 2):P * (i // 2) + P], ident[:])
                last.then_inc(v_filled, 1)


OUT_SHAPE = (1, 512, 1024)


def bucket_table():
    i = np.arange(DIFFS) - (S - 1)
    n = np.abs(i)
    log_ratio = (np.log(np.maximum(n, 1).astype(np.float32) / np.float32(8)) / np.float32(math.log(1024 / 8))).astype(np.float32)
    large = np.minimum(8 + (log_ratio * np.float32(8)).astype(np.int32), 15)
    bucket = np.where(i > 0, 16, 0) + np.where(n < 8, n, large)
    table = np.zeros((33, DIFFS), np.float32)
    table[bucket, np.arange(DIFFS)] = 1.0
    count = sum(((n % dil == 0) & (n // dil <= win // (2 * dil))).astype(np.int64) for win, dil in ((128, 1), (512, 4), (2048, 16)))
    table[32] = np.where(count > 0, np.log(np.maximum(count, 1)), -1e30)
    return table


def block2_tables():
    p = np.arange(P)
    width = np.array(GROUPS_W, np.float64)[2 * np.arange(2)[None, :] + (p >= 64)[:, None]]
    j = np.arange(PADW)
    corr = width[:, :, None] / np.minimum(j + 1, width[:, :, None])
    x = np.arange(L2)
    gamma = 1.0 - 2.0 ** (-5.0 - np.arange(RH))
    dist = x[None, :] - p[:, None]
    decay = RK ** -0.5 * np.where(dist[:, None, :] >= 0, gamma[None, :, None] ** np.maximum(dist, 0)[:, None, :], 0.0)
    pos = np.concatenate([np.arange(META, L2), np.arange(META)]).astype(np.float32)
    half = RK // 2
    row = p % 64
    freq = (np.float32(10000.0) ** (-(row % half).astype(np.float32) / np.float32(half))).astype(np.float32)
    angle = (freq[:, None] * pos[None, :]).astype(np.float32).astype(np.float64)
    used = (row < RK)[:, None]
    rot = np.zeros((P, P))
    for base in (0, 64):
        for i in range(half):
            rot[base + i + half, base + i] = -1.0
            rot[base + i, base + i + half] = 1.0
    tri = np.where(p[None, :] <= p[:, None], 0.0, NEG)
    tables = {"const_winv": 1.0 / width, "const_wcorr": corr, "const_decay": decay, "const_cos": np.cos(angle) * used,
              "const_sin": np.sin(angle) * used, "const_rot": rot, "const_tri": tri}
    return {name: np.ascontiguousarray(t, dtype=np.float32) for name, t in tables.items()}


def kernel(**inputs):
    import concourse.bacc as bacc
    from concourse.bass_utils import run_bass_kernel_spmd

    nc = bacc.Bacc("TRN2", target_bir_lowering=False, num_devices=1)
    consts = {"const_buckets": bucket_table(), "const_ones": np.ones((1, P), np.float32)} | block2_tables()
    arrays, aps = {}, {}
    for name, value in list(inputs.items()) + list(consts.items()):
        value = np.ascontiguousarray(value)
        arrays[name] = value
        aps[name] = nc.dram_tensor(name, value.shape, mybir.dt.from_np(value.dtype), kind="ExternalInput").ap()
    out = nc.dram_tensor("result", OUT_SHAPE, F32, kind="ExternalOutput").ap()
    program(nc, aps, out)
    result = run_bass_kernel_spmd(nc, [arrays], core_ids=[0])
    return result.results[0]["result"]
```
